# Optimizing a Trainium2 kernel written in Bass

```python
import jax, jax.numpy as jnp
from jax import lax
import numpy as np

D_MODEL = 4096
BATCH = 1
SEQ = 256
DEPTH = 1

D_MIX = D_MODEL
W_LRU = D_MIX // 2
W_ATT = D_MIX - W_LRU
LRU_BLOCKS = 16
LRU_BW = W_LRU // LRU_BLOCKS
CONV_W = 4
C_RG = 8.0
N_HEADS = 16
HEAD_DIM = W_ATT // N_HEADS
GRID_W = 64
WIN_R = 8
WIN_C = 16
EPS = 1e-6
D_IN = 2 * W_LRU + 4 * W_ATT

kernel_name = "hybrid_rglru_natten_parallel_heads"

def rms_norm(x, g):
    x32 = x.astype(jnp.float32)
    y = x32 * lax.rsqrt(jnp.mean(x32 * x32, axis=-1, keepdims=True) + EPS)
    return (y * g.astype(jnp.float32)).astype(x.dtype)

def _lin_combine(left, right):
    a_l, b_l = left
    a_r, b_r = right
    return a_l * a_r, a_r * b_l + b_r

def rglru_bidir(xa, conv_w, conv_b, wa, ba, wx, bx, lam):
    B, S, W = xa.shape
    xp = jnp.pad(xa, ((0, 0), (CONV_W // 2, CONV_W - 1 - CONV_W // 2), (0, 0)))
    xc = sum(xp[:, j:j + S] * conv_w[j] for j in range(CONV_W)) + conv_b
    xb = xc.reshape(B, S, LRU_BLOCKS, LRU_BW)
    r = jax.nn.sigmoid((jnp.einsum('bsnk,enkj->ebsnj', xb, wa).reshape(2, B, S, W)
                        + ba[:, None, None]).astype(jnp.float32))
    i = jax.nn.sigmoid((jnp.einsum('bsnk,enkj->ebsnj', xb, wx).reshape(2, B, S, W)
                        + bx[:, None, None]).astype(jnp.float32))
    log_a = -C_RG * r * jax.nn.softplus(-lam.astype(jnp.float32))[:, None, None]
    a = jnp.exp(log_a)
    b = jnp.sqrt(-jnp.expm1(2.0 * log_a)) * (i * xc.astype(jnp.float32)[None])
    _, h_f = lax.associative_scan(_lin_combine, (a[0], b[0]), axis=1)
    _, h_b = lax.associative_scan(_lin_combine, (a[1], b[1]), axis=1, reverse=True)
    return (h_f + h_b).astype(xa.dtype)

def neighbourhood_attention(q, k, v, rpb):
    B, S, H, Dh = q.shape
    rows = S // GRID_W
    kr = min(WIN_R, rows)
    kc = WIN_C
    scale = Dh ** -0.5
    qg = q.reshape(B, rows, GRID_W, H, Dh)
    kg = k.reshape(B, rows, GRID_W, H, Dh)
    vg = v.reshape(B, rows, GRID_W, H, Dh)
    col = jnp.arange(GRID_W)
    c_start = jnp.clip(col - kc // 2, 0, GRID_W - kc)
    col_idx = c_start[:, None] + jnp.arange(kc)
    col_off = col_idx - col[:, None] + (WIN_C - 1)

    def row_block(args):
        r, q_row = args
        r_start = jnp.clip(r - kr // 2, 0, rows - kr)
        row_idx = r_start + jnp.arange(kr)
        ridx = row_idx[:, None, None]
        cidx = col_idx[None]
        kb = kg[:, ridx, cidx]
        vb = vg[:, ridx, cidx]
        row_off = row_idx - r + (WIN_R - 1)
        bias = rpb[:, row_off[:, None, None], col_off[None]]
        bias = jnp.transpose(bias, (0, 2, 1, 3)).astype(jnp.float32)
        s = jnp.einsum('bchd,bkcwhd->bhckw', q_row, kb).astype(jnp.float32) * scale + bias
        p = jax.nn.softmax(s.reshape(B, H, GRID_W, kr * kc), axis=-1)
        p = p.reshape(B, H, GRID_W, kr, kc).astype(v.dtype)
        return jnp.einsum('bhckw,bkcwhd->bchd', p, vb)

    out = lax.map(row_block, (jnp.arange(rows), jnp.moveaxis(qg, 1, 0)))
    return jnp.moveaxis(out, 0, 1).reshape(B, S, H * Dh)

def hybrid_layer(x, cond, norm_g, w_ada, b_ada, w_in, conv_w, conv_b, lru_wa, lru_ba,
                 lru_wx, lru_bx, lru_lambda, rpb, gn_lru, gn_att, w_out):
    B, S, D = x.shape
    mod = cond @ w_ada + b_ada
    shift, scl, gate = jnp.split(mod, 3, axis=-1)
    h = rms_norm(x, norm_g) * (1.0 + scl[:, None]) + shift[:, None]
    p = h @ w_in
    cuts = [W_LRU, 2 * W_LRU, 2 * W_LRU + W_ATT, 2 * W_LRU + 2 * W_ATT, 2 * W_LRU + 3 * W_ATT]
    xa, ga, q, k, v, gb = jnp.split(p, cuts, axis=-1)
    ya = rglru_bidir(xa, conv_w, conv_b, lru_wa, lru_ba, lru_wx, lru_bx, lru_lambda)
    ya = rms_norm(ya, gn_lru) * jax.nn.silu(ga)
    yb = neighbourhood_attention(q.reshape(B, S, N_HEADS, HEAD_DIM),
                                 k.reshape(B, S, N_HEADS, HEAD_DIM),
                                 v.reshape(B, S, N_HEADS, HEAD_DIM), rpb)
    yb = rms_norm(yb, gn_att) * jax.nn.silu(gb)
    y = jnp.concatenate([ya, yb], axis=-1) @ w_out
    return x + gate[:, None] * y

def setup_inputs(seed: int = 0) -> dict:
    key = jax.random.key(seed)
    ks = jax.random.split(key, 20)
    nrm = jax.random.normal
    f32 = jnp.float32
    u = jax.random.uniform(ks[12], (DEPTH, 2, W_LRU), f32, 0.9, 0.999)
    a0 = u ** (1.0 / C_RG)
    return {
        "x": nrm(ks[0], (BATCH, SEQ, D_MODEL), f32),
        "c": nrm(ks[1], (BATCH, D_MODEL), f32),
        "norm_g": 1.0 + 0.01 * nrm(ks[2], (DEPTH, D_MODEL), f32),
        "w_ada": nrm(ks[3], (DEPTH, D_MODEL, 3 * D_MODEL), f32) * (0.5 * D_MODEL ** -0.5),
        "b_ada": 0.01 * nrm(ks[4], (DEPTH, 3 * D_MODEL), f32),
        "w_in": nrm(ks[5], (DEPTH, D_MODEL, D_IN), f32) * D_MODEL ** -0.5,
        "conv_w": nrm(ks[6], (DEPTH, CONV_W, W_LRU), f32) * CONV_W ** -0.5,
        "conv_b": 0.01 * nrm(ks[7], (DEPTH, W_LRU), f32),
        "lru_wa": nrm(ks[8], (DEPTH, 2, LRU_BLOCKS, LRU_BW, LRU_BW), f32) * LRU_BW ** -0.5,
        "lru_ba": 0.01 * nrm(ks[9], (DEPTH, 2, W_LRU), f32),
        "lru_wx": nrm(ks[10], (DEPTH, 2, LRU_BLOCKS, LRU_BW, LRU_BW), f32) * LRU_BW ** -0.5,
        "lru_bx": 0.01 * nrm(ks[11], (DEPTH, 2, W_LRU), f32),
        "lru_lambda": jnp.log(a0) - jnp.log1p(-a0),
        "rpb": 0.1 * nrm(ks[13], (DEPTH, N_HEADS, 2 * WIN_R - 1, 2 * WIN_C - 1), f32),
        "gn_lru": 1.0 + 0.01 * nrm(ks[14], (DEPTH, W_LRU), f32),
        "gn_att": 1.0 + 0.01 * nrm(ks[15], (DEPTH, W_ATT), f32),
        "w_out": nrm(ks[16], (DEPTH, D_MIX, D_MODEL), f32) * D_MIX ** -0.5,
        "final_g": 1.0 + 0.01 * nrm(ks[17], (D_MODEL,), f32),
    }

def reference(x, c, norm_g, w_ada, b_ada, w_in, conv_w, conv_b, lru_wa, lru_ba, lru_wx,
              lru_bx, lru_lambda, rpb, gn_lru, gn_att, w_out, final_g):
    cond = jax.nn.silu(c)
    for l in range(DEPTH):
        x = hybrid_layer(x, cond, norm_g[l], w_ada[l], b_ada[l], w_in[l], conv_w[l], conv_b[l],
                         lru_wa[l], lru_ba[l], lru_wx[l], lru_bx[l], lru_lambda[l], rpb[l],
                         gn_lru[l], gn_att[l], w_out[l])
    return rms_norm(x, final_g)


_drawn_inputs = setup_inputs


def setup_inputs(seed=0):
    import zlib

    import numpy as np

    out = dict(_drawn_inputs(seed))
    spreads = {}
    factors = {'norm_g': 8.0,
     'b_ada': 6.088,
     'conv_b': 8.0,
     'lru_wa': 3.927,
     'lru_ba': 64.0,
     'lru_bx': 64.0,
     'rpb': 7.263,
     'gn_lru': 62.898,
     'gn_att': 62.475,
     'final_g': 31.851}
    for name, (base, spread) in spreads.items():
        noise = np.random.default_rng([zlib.crc32(name.encode()), seed]).standard_normal(out[name].shape)
        drawn = base * np.exp(spread * noise) if base else spread * noise
        out[name] = __import__('jax').numpy.asarray(drawn.astype(out[name].dtype))
    for name, factor in factors.items():
        out[name] = (out[name] * factor).astype(out[name].dtype)
    return out
```

```python
from concourse import mybir
import concourse.bass as bass

ALU = mybir.AluOpType
ACT = mybir.ActivationFunctionType
AX = mybir.AxisListType.X
F32 = mybir.dt.float32
F32R = mybir.dt.float32r

P = 128
D = 4096
S = 256
TOK = S // P
W = 2048
D_IN = 6 * W
NB = 16
CONV_W = 4
C_RG = 8.0
NH = 16
GW = 64
ROWS = S // GW
WIN_R, WIN_C = 8, 16
NRO = 2 * ROWS - 1
RPB_W = 2 * WIN_C - 1
RO0 = WIN_R - ROWS
EPS = 1e-6
MASK = -1e30
SCALE = float(P) ** -0.5

NSB = 4
KT = D // P // NSB
SBW = KT * P
CT = 512
NT = D_IN // CT
GK = 2
GPT = KT // GK
WCH = 2
NW = 3
NG = 3
NA = 2
TPI = 3
NI = NT // TPI
API = 4
APS = NI * API
GSB = NT * GPT
NCO = D // CT
GPO = W // P // GK
GOUT = 2 * NCO * GPO
QB, KB, VB, GB, XB, GA = 8, 12, 16, 20, 0, 4
LAST = [QB, KB, VB, QB + 1, KB + 1, VB + 1, QB + 2, KB + 2, VB + 2, QB + 3, KB + 3, VB + 3,
        GB, GB + 1, GB + 2, GB + 3, 0, 1, 2, 3, GA, GA + 1, GA + 2, GA + 3]

C_C, C_NG, C_BSH, C_BSC = 0, 32, 64, 96
C_CW, C_CB, C_GNL, C_BA = 128, 192, 208, 224
C_BX, C_LAM, C_GNA = 256, 288, 320
NPAR = 336


def build(nc, x, c, norm_g, w_ada, b_ada, w_in, conv_w, conv_b, lru_wa, lru_ba, lru_wx, lru_bx,
          lru_lambda, rpb, gn_lru, gn_att, w_out, final_g, out):
    top = [(nc.sbuf_base + 31) // 32 * 32]

    def region(size):
        at = top[0]
        top[0] += (size + 31) // 32 * 32
        assert top[0] <= nc.sbuf_usable_end, top[0]
        return at

    def place(name, shape, at, dt=F32):
        return nc.alloc_sbuf_tensor_at(name, [P] + shape, dt, offset=at)

    def sem(name):
        return nc.alloc_semaphore(name)

    TB = TOK * CT * 4
    at_p = region(NT * TB)
    at_h = region(2 * KT * S * 4)
    at_xs = region(TOK * SBW * 4)
    at_h32 = region(KT * S * 4)
    at_mod = region(2 * SBW * 4)
    at_wst = region(NW * WCH * GK * CT * 4)
    at_ast = region(NA * 2 * SBW * 4)
    at_whi = region(NG * GK * CT * 4)
    at_wlo = region(NG * GK * CT * 4)

    proj = place("proj", [NT, TOK, CT], at_p)
    h_hi = place("h_hi", [KT, S], at_h, F32R)
    h_lo = place("h_lo", [KT, S], at_h + KT * S * 4, F32R)
    xs = place("xs", [TOK, SBW], at_xs)
    h32 = place("h32", [KT, S], at_h32)
    mod = place("mod", [2, SBW], at_mod)
    w_st = place("w_st", [NW, WCH, GK, CT], at_wst)
    a_st = place("a_st", [NA, 2, SBW], at_ast)
    w_hi = place("w_hi", [NG, GK, CT], at_whi, F32R)
    w_lo = place("w_lo", [NG, GK, CT], at_wlo, F32R)
    xfull = place("xfull", [TOK, D], at_p)
    maskfill = place("maskfill", [GW * NH * NRO * GW // P], at_p + GB * TB)
    qkT = place("qkT", [2, S], at_xs)
    prob = place("prob", [2, TOK, S], at_xs + 2048)
    probT = place("probT", [2, S], at_xs + 6144)
    bias = place("bias", [2, TOK, S], at_h32)
    sig = place("sig", [TOK, CT], at_h32 + 4096)
    yB_hi = place("yB_hi", [NH, S], at_p + KB * TB, F32R)
    yB_lo = place("yB_lo", [NH, S], at_p + VB * TB, F32R)
    yA_hi = place("yA_hi", [NB, S], at_p + XB * TB, F32R)
    yA_lo = place("yA_lo", [NB, S], at_p + GA * TB, F32R)
    XPAD = S + 4
    xaT = place("xaT", [4, XPAD], at_h)
    gaS = place("gaS", [4, S], at_h + 4160)
    xc = place("xc", [2, S], at_h + 8256)
    hsq = place("hsq", [2, S], at_h + 10304)
    hacc = place("hacc", [2, S], at_h + 12352)
    gate_wt = place("gate_wt", [2, 2, 2, P], at_xs)
    rv = place("rv", [2, 2, S], at_xs + 4096)
    ib = place("ib", [2, 2, S], at_h32)
    wa_ = place("wa_", [2, 2, S], at_h32 + 4096)
    hh = place("hh", [2, 2, S], at_ast)
    fing = place("fing", [D], at_h)
    xres = place("xres", [2, TOK, CT], at_h32)
    mod2 = place("mod2", [2, SBW], at_xs)
    ident = place("ident", [P], region(512))
    ones = place("ones", [P], region(512))
    par_rows = place("par_rows", [3, P], region(1536))
    par = place("par", [NPAR], region(NPAR * 4))
    cond = place("cond", [32], region(128))
    mcols = place("mcols", [3, KT], region(96))
    coef = place("coef", [32], region(128))
    tl = place("tl", [5, 32], region(640))
    st = place("st", [64], region(256))
    fss = place("fss", [TOK, NCO], region(64))
    mx = place("mx", [2, TOK], region(32))
    es = place("es", [4, TOK], region(32))
    ST_SS, ST_RT, ST_R, ST_EPS, ST_B, ST_BR, ST_A, ST_AR, ST_F, ST_FR = 0, 2, 4, 6, 8, 10, 12, 14, 16, 18

    banks = [nc.alloc_psum_tensor(f"bank{i}", [P, 512], F32) for i in range(8)]
    acc = [banks[0:2], banks[2:4], banks[4:6]]
    side = [banks[6], banks[7], banks[4], banks[5]]

    bias_img = nc.dram_tensor("bias_img", (GW, NH, NRO, GW), F32, kind="Internal").ap()

    w_landed = [sem(f"w_landed{i}") for i in range(NW)]
    a_landed = [sem(f"a_landed{i}") for i in range(NA)]
    hi_ready, lo_ready, gran_used = sem("hi_ready"), sem("lo_ready"), sem("gran_used")
    evac_done, ada_step = sem("evac_done"), sem("ada_step")
    mod_ps, mod_cols, xs_landed, xs_scaled = sem("mod_ps"), sem("mod_cols"), sem("xs_landed"), sem("xs_scaled")
    xT_ps, h32_ready, hh_ready, hl_ready = sem("xT_ps"), sem("h32_ready"), sem("hh_ready"), sem("hl_ready")
    par_landed, par_ps, par_ready, cond_ready = sem("par_landed"), sem("par_ps"), sem("par_ready"), sem("cond_ready")
    consts_ready, x_landed, rstd_ready = sem("consts_ready"), sem("x_landed"), sem("rstd_ready")
    coef_ready, eps_ready = sem("coef_ready"), sem("eps_ready")
    mask_set, mask_stored, img_stored = sem("mask_set"), sem("mask_stored"), sem("img_stored")
    bias_landed = [sem("bias_landed0"), sem("bias_landed1")]
    qkT_ps, qkT_ready, s_ps, s_ready = sem("qkT_ps"), sem("qkT_ready"), sem("s_ps"), sem("s_ready")
    p_ready, pT_ps, pT_ready, o_ps, o_ready = sem("p_ready"), sem("pT_ps"), sem("pT_ready"), sem("o_ps"), sem("o_ready")
    rinv_ready = sem("rinv_ready")
    sig_ready, z_ready, yBT_ps, yB_hi_r, yB_lo_r = sem("sig_ready"), sem("z_ready"), sem("yBT_ps"), sem("yB_hi_r"), sem("yB_lo_r")
    rB_ready, rA_ready = sem("rB_ready"), sem("rA_ready")
    xaT_ps, gaT_ps, xaT_ready, gsig_ready, gaS_ready = sem("xaT_ps"), sem("gaT_ps"), sem("xaT_ready"), sem("gsig_ready"), sem("gaS_ready")
    pad_set, xc_ready, gate_ps, ri_ready, v_ready = sem("pad_set"), sem("xc_ready"), sem("gate_ps"), sem("ri_ready"), sem("v_ready")
    gwt_landed = sem("gwt_landed")
    w_ready, sq_ready, scan_ready, h_ready, y_ready = sem("w_ready"), sem("sq_ready"), sem("scan_ready"), sem("h_ready"), sem("y_ready")
    yA_hi_r, yA_lo_r, hacc_ready, ssA_ps = sem("yA_hi_r"), sem("yA_lo_r"), sem("hacc_ready"), sem("ssA_ps")
    hsq_ready = sem("hsq_ready")
    gzero, gbias_landed, gate_bc_ps, gate_ready = sem("gzero"), sem("gbias_landed"), sem("gate_bc_ps"), sem("gate_ready")
    fing_landed, sq_used = sem("fing_landed"), sem("sq_used")
    xres_landed = [sem("xres_landed0"), sem("xres_landed1")]
    t3_ready, fss_ready, t4_ready, rF_ready, fin_ready, out_stored = (
        sem("t3_ready"), sem("fss_ready"), sem("t4_ready"), sem("rF_ready"), sem("fin_ready"), sem("out_stored"))
    sigc_ready, xroot_ready, lam_ready, elam_ready, fsum_ready = (
        sem("sigc_ready"), sem("xroot_ready"), sem("lam_ready"), sem("elam_ready"), sem("fsum_ready"))
    dve_step, act_step, pool_step = sem("dve_step"), sem("act_step"), sem("pool_step")

    x_v = x.rearrange("b (t p) d -> p (b t) d", p=P)
    out_v = out.rearrange("b (t p) d -> p (b t) d", p=P)
    w_in_v = w_in.rearrange("l (k p) n -> p (l k) n", p=P)
    w_ada_v = w_ada.rearrange("l (k p) n -> p (l k) n", p=P)
    w_out_v = w_out.rearrange("l (k p) n -> p (l k) n", p=P)
    b_gate = b_ada[:, 2 * D:3 * D]

    def gran_of_tile(t):
        return GPT * t

    def chunk_wait(eng, wc_slot, n):
        eng.wait_ge(w_landed[wc_slot], n)

    def proj_at(t, tok=None):
        if isinstance(t, int):
            v = proj[:, t, :, :]
        else:
            v = proj[:, bass.ds(t, 1), :, :].rearrange("p a t n -> p (a t) n")
        return v if tok is None else v[:, tok, :]

    def head(part, h, tok):
        return proj[:, part + h // 4, tok, (h % 4) * P:(h % 4 + 1) * P]

    def out_tile(o):
        return proj[:, (QB + o) if o < 4 else (GB + o - 4), :, :]

    block = nc.Block()
    with block:
        @block.sync
        def _(sp):
            def w_in_chunk(s, i, tile_col, u, half):
                base = s * NT * 2 + 2 * u + half
                n = i * (2 * TPI) + base
                if not (isinstance(n, int) and n < NW):
                    sp.wait_ge(lo_ready, n * 2 - 4)
                k0 = s * KT + half * WCH * GK
                src = w_in_v[:, k0:k0 + WCH * GK, bass.ds(tile_col * CT, CT)]
                sp.dma_start(w_st[:, base % NW, :, :, :].rearrange("p a b n -> p (a b) n"), src).then_inc(w_landed[base % NW], 16)

            def ada_chunk(n, j2, col):
                if not (isinstance(n, int) and n < NA):
                    sp.wait_ge(ada_step, n * 2 - 2)
                slot = n % NA if isinstance(n, int) else None
                return slot

            def ada_dma(n0, i, q, col0):
                n = i * API + (n0 + q)
                if not (isinstance(n, int) and n < NA):
                    sp.wait_ge(ada_step, n * 2 - 2)
                j2 = i * (API // 2) + q // 2
                src = w_ada_v[:, bass.ds(j2 * 2, 2), col0:col0 + SBW]
                sp.dma_start(a_st[:, q % NA, :, :], src).then_inc(a_landed[q % NA], 16)

            def ada_col(s, q):
                return (D if q % 2 == 0 else 0) + s * SBW

            for i in range(NI):
                for q in range(API):
                    ada_dma(0, i, q, ada_col(0, q))

            def step(s, i):
                for u in range(TPI):
                    for half in range(2):
                        n = 2 * u + half
                        if n < API:
                            ada_dma((s + 1) * APS, i, n, ada_col(s + 1, n))
                        w_in_chunk(s, i, i * TPI + u, u, half)

            for s in range(NSB - 1):
                step(s, 0)
                with sp.Fori(1, NI) as i:
                    step(s, i)
            s = NSB - 1
            for t in range(NT):
                for half in range(2):
                    n = 2 * t + half
                    if n == 0:
                        sp.wait_ge(gbias_landed, 16)
                    if n < APS:
                        ada_dma(NSB * APS, n // API, n % API, 2 * D + (n % 2) * SBW)
                    w_in_chunk(s, t // TPI, LAST[t], t % TPI, half)
            for n in range(GOUT // WCH):
                tile, half = n // (GPO // WCH), n % (GPO // WCH)
                wc = NSB * NT * 2 + n
                sp.wait_ge(lo_ready, wc * 2 - 4)
                k0 = (W // P if tile < NCO else 0) + half * WCH * GK
                sp.dma_start(w_st[:, wc % NW, :, :, :].rearrange("p a b n -> p (a b) n"),
                             w_out_v[:, k0:k0 + WCH * GK, (tile % NCO) * CT:(tile % NCO + 1) * CT]).then_inc(w_landed[wc % NW], 16)
                m = gate_chunk_at(n)
                for q in m:
                    cn = (NSB + 1) * APS + q
                    sp.wait_ge(ada_step, cn * 2 - 2)
                    if q == 0:
                        sp.wait_ge(hsq_ready, NB // 2)
                        sp.wait_ge(yA_lo_r, NB // 2)
                    j2 = q % (APS // 2)
                    col = 2 * D + (2 + q // (APS // 2)) * SBW
                    sp.dma_start(a_st[:, cn % NA, :, :], w_ada_v[:, 2 * j2:2 * j2 + 2, col:col + SBW]).then_inc(a_landed[cn % NA], 16)
            for t in range(NCO):
                sp.wait_ge(fin_ready, t + 1)
                sp.dma_start(out_v[:, :, t * CT:(t + 1) * CT], out_tile(t)).then_inc(out_stored, 16)
            sp.wait_ge(out_stored, 16 * NCO)

        @block.gpsimd
        def _(pool):
            steps = [0]

            def link(ins):
                steps[0] += 1
                ins.then_inc(pool_step, 1)
                pool.wait_ge(pool_step, steps[0])

            pool.memset(st[:, ST_EPS:ST_EPS + 1], EPS).then_inc(eps_ready, 1)
            link(pool.memset(ident[:], 0.0))
            pool.affine_select(out=ident[:], in_=ident[:], compare_op=ALU.not_equal, fill=1.0, base=0,
                               pattern=[[-1, P]], channel_multiplier=1).then_inc(consts_ready, 1)
            pool.memset(ones[:], 1.0).then_inc(consts_ready, 1)
            pool.dma_start(xfull[:], x_v).then_inc(x_landed, 16)
            pool.dma_start(xs[:], x_v[:, :, 0:SBW]).then_inc(xs_landed, 16)
            pool.memset(maskfill[:], MASK).then_inc(mask_set, 1)
            pool.wait_ge(mask_set, 1)
            pool.dma_start(bias_img.rearrange("c h r k -> (c h r k)").rearrange("(p n) -> p n", p=P),
                           maskfill[:]).then_inc(mask_stored, 16)

            def scale_xs(s):
                pool.wait_ge(xs_landed, 16 * (s + 1))
                pool.wait_ge(rstd_ready, 1)
                for tok in range(TOK):
                    pool.tensor_scalar(xs[:, tok, :], xs[:, tok, :], st[:, ST_R + tok:ST_R + tok + 1], None,
                                       ALU.mult).then_inc(xs_scaled, 1)

            scale_xs(0)
            pool.wait_ge(mask_stored, 16)
            img = bias_img
            HALF = WIN_C // 2
            last_c = GW - WIN_C
            n_store = 0
            for ro in range(NRO):
                tab = rpb[0, :, RO0 + ro, :]
                for c0, nc_, tstep, istep, t0, k0 in (
                    (0, HALF, -1, 0, WIN_C - 1, 0),
                    (HALF, last_c + 1, 0, 1, WIN_C - 1 - HALF, 0),
                    (last_c + HALF + 1, HALF - 1, -1, 0, WIN_C - 1 - HALF - 1, last_c),
                ):
                    src = bass.AP(tensor=tab.tensor, offset=tab.offset + t0,
                                  ap=[[tab.ap[0][0], NH], [tstep, nc_], [1, WIN_C]])
                    at = img[c0, 0, ro, k0:k0 + 1]
                    dst = bass.AP(tensor=img.tensor, offset=at.offset,
                                  ap=[[NRO * GW, NH], [NH * NRO * GW + istep, nc_], [1, WIN_C]])
                    pool.dma_start(dst, src).then_inc(img_stored, 16)
                    n_store += 1
            for s in range(1, NSB):
                pool.wait_ge(xT_ps, 4 * s)
                pool.dma_start(xs[:], x_v[:, :, s * SBW:(s + 1) * SBW]).then_inc(xs_landed, 16)
                scale_xs(s)
            pool.wait_ge(mod_ps, NSB)
            pool.memset(mod[:], 0.0).then_inc(gzero, 1)
            pool.wait_ge(gzero, 1)
            pool.dma_start(mod[0:1, :, :].rearrange("p a n -> p (a n)"), b_gate[:, 0:2 * SBW]).then_inc(gbias_landed, 16)
            pool.wait_ge(img_stored, 16 * n_store)
            pool.wait_ge(hl_ready, 4 * NSB)
            for h in range(NH):
                if h >= 2:
                    pool.wait_ge(s_ready, 2 * (h - 1))
                for r in range(ROWS):
                    pool.dma_start(bias[(r % 2) * GW:(r % 2 + 1) * GW, h % 2, r // 2, :].rearrange("p (a n) -> p a n", a=ROWS),
                                   bias_img[:, h, ROWS - 1 - r:2 * ROWS - 1 - r, :]).then_inc(bias_landed[h % 2], 16)
            pool.wait_ge(gran_used, NSB * GSB)
            pool.memset(xaT[:], 0.0).then_inc(pad_set, 1)
            pool.memset(hacc[:], 0.0).then_inc(pad_set, 1)
            pool.wait_ge(pad_set, 2)
            pool.wait_ge(yB_lo_r, NH // 2)
            for g in range(NB // 2):
                if g >= 1:
                    pool.wait_ge(gate_ps, g)
                for k, w in enumerate((lru_wa, lru_wx)):
                    for e in range(2):
                        pool.dma_start(gate_wt[:, k, e, :, :],
                                       w[0, e, 2 * g:2 * g + 2, :, :].rearrange("n k j -> k n j")).then_inc(gwt_landed, 16)
                pool.wait_ge(ri_ready, g + 1)
                for e in range(2):
                    pool.tensor_tensor(ib[:, e, :, :], ib[:, e, :, :], xc[:], ALU.mult).then_inc(sq_used, 1)
                pool.wait_ge(h_ready, g + 1)
                pool.tensor_tensor(hsq[:], hh[:, 0, :, :], hh[:, 0, :, :], ALU.mult).then_inc(hsq_ready, 1)
                pool.wait_ge(hsq_ready, g + 1)
                pool.tensor_tensor(hacc[:], hacc[:], hsq[:], ALU.add).then_inc(hacc_ready, 1)
                pool.wait_ge(hacc_ready, g + 1)
            pool.wait_ge(y_ready, NB // 2)
            pool.memset(mod2[:], 0.0).then_inc(gzero, 1)
            pool.wait_ge(gzero, 2)
            pool.dma_start(mod2[0:1, :, :].rearrange("p a n -> p (a n)"), b_gate[:, 2 * SBW:4 * SBW]).then_inc(gbias_landed, 16)
            pool.wait_ge(ssA_ps, 1)
            pool.dma_start(fing[:], final_g.rearrange("(a n) -> a n", a=1).to_broadcast([P, D])).then_inc(fing_landed, 16)
            for t in range(2):
                pool.dma_start(xres[:, t, :, :], x_v[:, :, t * CT:(t + 1) * CT]).then_inc(xres_landed[t], 16)
            for t in range(NCO):
                o = out_tile(t)
                gate = (mod if t < 4 else mod2)[:, (t % 4) // 2, (t % 2) * CT:(t % 2 + 1) * CT]
                pool.wait_ge(evac_done, NSB * NT + NCO + t + 1)
                pool.wait_ge(gate_ready, t + 1)
                for tok in range(TOK):
                    pool.tensor_tensor(o[:, tok, :], o[:, tok, :], gate, ALU.mult).then_inc(pool_step, 1)
                    steps[0] += 1
                pool.wait_ge(pool_step, steps[0])
                pool.wait_ge(xres_landed[t % 2], 16 * (t // 2 + 1))
                pool.tensor_tensor(o, o, xres[:, t % 2, :, :], ALU.add).then_inc(t3_ready, 1)
                if t + 2 < NCO:
                    pool.wait_ge(t3_ready, t + 1)
                    pool.dma_start(xres[:, t % 2, :, :], x_v[:, :, (t + 2) * CT:(t + 3) * CT]).then_inc(xres_landed[t % 2], 16)
                pool.wait_ge(fss_ready, 2 * t + 2)
                if t == 0:
                    pool.wait_ge(fing_landed, 16)
                for tok in range(TOK):
                    ins = pool.tensor_tensor(o[:, tok, :], o[:, tok, :], fing[:, t * CT:(t + 1) * CT], ALU.mult)
                ins.then_inc(t4_ready, 1)

        @block.scalar
        def _(act):
            steps = [0]

            def link(ins):
                steps[0] += 1
                ins.then_inc(act_step, 1)
                act.wait_ge(act_step, steps[0])

            def dma(dst, src):
                act.dma_start(dst, src).then_inc(par_landed, 16)

            r = par_rows
            dma(r[0:32, 0, :], c.rearrange("b (n p) -> (b n) p", p=P))
            dma(r[32:64, 0, :], norm_g.rearrange("l (n p) -> (l n) p", p=P))
            dma(r[64:128, 0, :], b_ada[:, 0:2 * D].rearrange("l (n p) -> (l n) p", p=P))
            dma(r[0:64, 1, :], conv_w.rearrange("l j (n p) -> (l j n) p", p=P))
            dma(r[64:80, 1, :], conv_b.rearrange("l (n p) -> (l n) p", p=P))
            dma(r[80:96, 1, :], gn_lru.rearrange("l (n p) -> (l n) p", p=P))
            dma(r[96:128, 1, :], lru_ba.rearrange("l e (n p) -> (l e n) p", p=P))
            dma(r[0:32, 2, :], lru_bx.rearrange("l e (n p) -> (l e n) p", p=P))
            dma(r[32:64, 2, :], lru_lambda.rearrange("l e (n p) -> (l e n) p", p=P))
            dma(r[64:80, 2, :], gn_att.rearrange("l (n p) -> (l n) p", p=P))
            act.wait_ge(par_ps, 1)
            act.copy(par[:], side[0][:, 0:NPAR]).then_inc(par_ready, 1)
            act.wait_ge(par_ready, 1)
            act.activation(cond[:], par[:, C_C:C_C + 32], ACT.Sigmoid).then_inc(sigc_ready, 1)
            act.wait_ge(x_landed, 16)
            for tok in range(TOK):
                link(act.activation(xfull[:, tok, :], xfull[:, tok, :], ACT.Square,
                                    accum_out=st[:, ST_SS + tok:ST_SS + tok + 1]))
            act.wait_ge(eps_ready, 1)
            act.activation(st[:, ST_RT:ST_RT + 2], st[:, ST_SS:ST_SS + 2], ACT.Sqrt,
                           bias=st[:, ST_EPS:ST_EPS + 1], scale=1.0 / D).then_inc(xroot_ready, 1)
            act.wait_ge(lam_ready, 1)
            act.activation(tl[:, 1, :], tl[:, 0, :], ACT.Exp, scale=-1.0).then_inc(elam_ready, 1)

            def split_hi(gr, slot_chunk, n_chunk, which, slot_gr, wait_used):
                if which == 0:
                    act.wait_ge(w_landed[slot_chunk], n_chunk)
                if wait_used:
                    act.wait_ge(gran_used, gr - (NG - 1))
                act.copy(w_hi[:, slot_gr, :, :], w_st[:, slot_chunk, which, :, :]).then_inc(hi_ready, 1)

            def split_h(s, g):
                if s > 0:
                    act.wait_ge(gran_used, s * GSB - GPT + g + 1)
                act.wait_ge(h32_ready, 4 * s + g + 1)
                act.copy(h_hi[:, 2 * g:2 * g + 2, :], h32[:, 2 * g:2 * g + 2, :]).then_inc(hh_ready, 1)

            def step(s, i, first):
                for u in range(TPI):
                    for g in range(GPT):
                        n = u * GPT + g
                        if first and n < 3:
                            for k in ((0, 1), (2,), (3,))[n]:
                                split_h(s, k)
                        c0 = s * NT * 2 + n // 2
                        gr = i * (TPI * GPT) + (s * GSB + n)
                        used = not (isinstance(gr, int) and gr < NG)
                        split_hi(gr, c0 % NW, (i * (2 * TPI // NW) + c0 // NW + 1) * 16, n % 2, n % NG, used)

            for s in range(NSB - 1):
                step(s, 0, True)
                with act.Fori(1, NI) as i:
                    step(s, i, False)

            def copy_qkT(h):
                act.wait_ge(qkT_ps, h + 1)
                if h >= 1:
                    act.wait_ge(s_ps, h)
                act.copy(qkT[:].rearrange("p a n -> p (a n)"), side[2][:]).then_inc(qkT_ready, 1)

            def exps(h):
                act.wait_ge(s_ready, 2 * h + 2)
                for tok in range(TOK):
                    act.activation(prob[:, h % 2, tok, :], prob[:, h % 2, tok, :], ACT.Exp,
                                   bias=mx[:, h % 2, tok:tok + 1], accum_out=es[:, h % 4, tok:tok + 1]).then_inc(p_ready, 1)

            def copy_probT(h):
                act.wait_ge(pT_ps, h + 1)
                act.wait_ge(o_ps, h) if h >= 1 else None
                act.copy(probT[:].rearrange("p a n -> p (a n)"), side[0][:]).then_inc(pT_ready, 1)

            def scale_o(h):
                act.wait_ge(o_ps, h + 1)
                act.wait_ge(rinv_ready, h + 1)
                for tok in range(TOK):
                    ins = act.activation(head(QB, h, tok), side[1][:, tok * P:(tok + 1) * P], ACT.Copy,
                                         scale=es[:, h % 4, tok:tok + 1])
                ins.then_inc(o_ready, 1)

            def gate_sig(t):
                if t >= 1:
                    act.wait_ge(z_ready, t)
                act.activation(sig[:], proj[:, GB + t, :, :], ACT.Sigmoid).then_inc(sig_ready, 1)

            def norm_B():
                act.wait_ge(o_ready, NH)
                for tok in range(TOK):
                    link(act.activation(proj[:, VB:VB + 4, tok, :], proj[:, QB:QB + 4, tok, :], ACT.Square,
                                        accum_out=st[:, ST_B + tok:ST_B + tok + 1]))
                act.activation(st[:, ST_BR:ST_BR + 2], st[:, ST_B:ST_B + 2], ACT.Sqrt,
                               bias=st[:, ST_EPS:ST_EPS + 1], scale=1.0 / W).then_inc(rB_ready, 1)

            def yB_upper(r):
                act.wait_ge(yBT_ps, r + 1)
                for k in range(2):
                    n = 2 * r + k
                    ins = act.activation(yB_hi[:, n, :], side[2 + r % 2][:, k * S:(k + 1) * S], ACT.Copy,
                                         scale=par[:, C_GNA + n:C_GNA + n + 1])
                ins.then_inc(yB_hi_r, 1)

            s = NSB - 1
            for g in range(GSB):
                if g < 3:
                    for k in ((0, 1), (2,), (3,))[g]:
                        split_h(s, k)
                for h in range(NH):
                    if g == copy_qkT_at(h):
                        copy_qkT(h)
                    if g == exps_at(h):
                        exps(h)
                    if g == copy_probT_at(h):
                        copy_probT(h)
                    if g == scale_o_at(h):
                        scale_o(h)
                if g == NORM_B_AT:
                    norm_B()
                if GATE_AT <= g < GATE_AT + 4:
                    gate_sig(g - GATE_AT)
                for r in range(NH // 2):
                    if g == yBT_AT + r + 1:
                        yB_upper(r)
                c0 = s * NT * 2 + g // 2
                split_hi(s * GSB + g, c0 % NW, (c0 // NW + 1) * 16, g % 2, g % NG, True)

            def lru_transposed(q):
                act.wait_ge(xaT_ps, q + 1)
                if q == 0:
                    act.wait_ge(pad_set, 2)
                else:
                    act.wait_ge(xc_ready, 2 * q)
                for b in range(2):
                    ins = act.copy(xaT[:, 2 * b:2 * b + 2, 2:2 + S], side[b][:].rearrange("p (k n) -> p k n", k=2))
                ins.then_inc(xaT_ready, 1)

            def lru_gate_sigmoids(q):
                act.wait_ge(gaT_ps, q + 1)
                if q > 0:
                    act.wait_ge(y_ready, 2 * q)
                for b in range(2):
                    ins = act.activation(gaS[:, 2 * b:2 * b + 2, :], side[2 + b][:].rearrange("p (k n) -> p k n", k=2), ACT.Sigmoid)
                ins.then_inc(gsig_ready, 1)

            def lru_sigmoids(g):
                act.wait_ge(gate_ps, g + 1)
                if g >= 1:
                    act.wait_ge(scan_ready, 4 * g)
                for e in range(2):
                    for k in range(2):
                        n = e * NB + 2 * g + k
                        act.activation(rv[:, e, k, :], side[2 * e][:, k * S:(k + 1) * S], ACT.Sigmoid,
                                       bias=par[:, C_BA + n:C_BA + n + 1]).then_inc(act_step, 1)
                        steps[0] += 1
                        ins = act.activation(ib[:, e, k, :], side[2 * e + 1][:, k * S:(k + 1) * S], ACT.Sigmoid,
                                             bias=par[:, C_BX + n:C_BX + n + 1])
                ins.then_inc(ri_ready, 1)
                act.wait_ge(act_step, steps[0])
                act.wait_ge(coef_ready, 1)
                for e in range(2):
                    for k in range(2):
                        n = e * NB + 2 * g + k
                        ins = act.activation(rv[:, e, k, :], rv[:, e, k, :], ACT.Tanh, scale=coef[:, n:n + 1])
                ins.then_inc(v_ready, 1)

            def lru_root(g):
                act.wait_ge(v_ready, g + 1)
                act.wait_ge(w_ready, 2 * g + 1)
                act.activation(rv[:], rv[:], ACT.Sqrt).then_inc(sq_ready, 1)

            def yA_upper(g):
                act.wait_ge(y_ready, g + 1)
                act.wait_ge(xaT_ready, g // 2 + 1)
                act.copy(yA_hi[:, 2 * g:2 * g + 2, :], hh[:, 1, :, :]).then_inc(yA_hi_r, 1)

            def norm_A():
                act.wait_ge(ssA_ps, 1)
                act.activation(st[:, ST_AR:ST_AR + 2], side[0][:, 0:2], ACT.Sqrt,
                               bias=st[:, ST_EPS:ST_EPS + 1], scale=1.0 / W).then_inc(rA_ready, 1)

            def gate_copy(n):
                act.wait_ge(gate_bc_ps, n + 1)
                m = mod if n < 4 else mod2
                act.copy(m[:, (n % 4) // 2, (n % 2) * CT:(n % 2 + 1) * CT], side[1 + n % 3][:]).then_inc(gate_ready, 1)

            def squares(t):
                act.wait_ge(t3_ready, t + 1)
                for tok in range(TOK):
                    if t + tok > 0:
                        act.wait_ge(fss_ready, 2 * t + tok)
                    act.activation(side[0][:], out_tile(t)[:, tok, :], ACT.Square,
                                   accum_out=fss[:, tok, t:t + 1]).then_inc(fss_ready, 1)

            for g in range(GOUT):
                for q in range(NB // 4):
                    if g == 16 * q + 3:
                        lru_transposed(q)
                    if g == 16 * q + 5:
                        lru_gate_sigmoids(q)
                for n in range(NB // 2):
                    if g == 8 * n + 9:
                        lru_sigmoids(n)
                    if g == 8 * n + 11:
                        lru_root(n)
                    if g == 8 * n + 13:
                        yA_upper(n)
                if g == NORM_A_AT + 3:
                    norm_A()
                for n in range(NCO):
                    if g == gate_bc_at(n) + 3:
                        gate_copy(n)
                    if g == evac_at(NCO + n) + 3:
                        squares(n)
                wc = NSB * NT * 2 + g // 2
                split_hi(NSB * GSB + g, wc % NW, (wc // NW + 1) * 16, g % 2, g % NG, True)
            squares(NCO - 1)
            act.wait_ge(fsum_ready, 1)
            act.activation(st[:, ST_FR:ST_FR + 2], st[:, ST_F:ST_F + 2], ACT.Sqrt,
                           bias=st[:, ST_EPS:ST_EPS + 1], scale=1.0 / D).then_inc(rF_ready, 1)

        @block.vector
        def _(dve):
            steps = [0]

            def link(ins):
                steps[0] += 1
                ins.then_inc(dve_step, 1)
                dve.wait_ge(dve_step, steps[0])

            dve.wait_ge(sigc_ready, 1)
            dve.tensor_tensor(cond[:], cond[:], par[:, C_C:C_C + 32], ALU.mult).then_inc(cond_ready, 1)
            dve.wait_ge(cond_ready, 1)
            lam = par[:, C_LAM:C_LAM + 32]
            dve.scalar_tensor_tensor(out=tl[:, 0, :], in0=lam, scalar=-1.0, in1=lam, op0=ALU.mult, op1=ALU.max).then_inc(lam_ready, 1)

            def ada(n, slot, k, acc_t, which, jj, cnd, first, n_land):
                if jj == 0:
                    dve.wait_ge(a_landed[slot], n_land)
                if first:
                    dve.tensor_scalar(acc_t[:, which, :], a_st[:, slot, jj, :], cnd, None, ALU.mult).then_inc(ada_step, 1)
                    return
                dve.wait_ge(ada_step, n - 2 * (jj == 0) if k else n)
                dve.scalar_tensor_tensor(out=acc_t[:, which, :], in0=a_st[:, slot, jj, :], scalar=cnd,
                                         in1=acc_t[:, which, :], op0=ALU.mult, op1=ALU.add).then_inc(ada_step, 1)

            def ada_pair(s, i, q):
                for jj in range(2):
                    n = i * (2 * API) + (s * APS * 2 + 2 * q + jj)
                    j = i * API + (q // 2 * 2 + jj)
                    first = isinstance(i, int) and i == 0 and q < 2 and jj == 0
                    if first and s > 0:
                        dve.wait_ge(mod_ps, s)
                    cnd = cond[:, j:j + 1] if isinstance(j, int) else cond[:, bass.ds(j, 1)]
                    ada(n, q % NA, 1, mod, q % 2, jj, cnd, first, (i * (API // NA) + ((s * APS + q) // NA + 1)) * 16)

            def split_lo(gr, slot_chunk, which, slot_gr):
                dve.wait_ge(hi_ready, gr + 1)
                dve.tensor_tensor(w_lo[:, slot_gr, :, :], w_st[:, slot_chunk, which, :, :],
                                  w_hi[:, slot_gr, :, :].bitcast(F32), ALU.subtract).then_inc(lo_ready, 1)

            def split_h(s, g):
                dve.wait_ge(hh_ready, 4 * s + g + 1)
                dve.tensor_tensor(h_lo[:, 2 * g:2 * g + 2, :], h32[:, 2 * g:2 * g + 2, :],
                                  h_hi[:, 2 * g:2 * g + 2, :].bitcast(F32), ALU.subtract).then_inc(hl_ready, 1)

            def evac(s, t, tile, buf):
                n = t + s * NT
                dve.wait_ge(gran_used, n * GPT + GPT)
                if s > 0:
                    dve.wait_ge(evac_done, n - (NT - 1) if s < NSB - 1 else NT * (NSB - 1))
                for tok in range(TOK):
                    if s == 0:
                        ins = dve.tensor_copy(proj_at(tile, tok), acc[buf][tok][:])
                    else:
                        ins = dve.tensor_tensor(proj_at(tile, tok), proj_at(tile, tok), acc[buf][tok][:], ALU.add)
                ins.then_inc(evac_done, 1)

            def mod_columns(s):
                dve.wait_ge(mod_ps, s + 1)
                b0 = s * KT
                link(dve.tensor_tensor(mcols[:, 2, :], side[0][:, 0:KT], par[:, C_BSC + b0:C_BSC + b0 + KT], ALU.add))
                dve.tensor_tensor(mcols[:, 1, :], side[0][:, KT:2 * KT], par[:, C_BSH + b0:C_BSH + b0 + KT], ALU.add).then_inc(mod_cols, 1)
                dve.scalar_tensor_tensor(out=mcols[:, 0, :], in0=mcols[:, 2, :], scalar=1.0,
                                         in1=par[:, C_NG + b0:C_NG + b0 + KT], op0=ALU.add, op1=ALU.mult).then_inc(mod_cols, 1)
                dve.wait_ge(mod_cols, 2 * s + 2)

            def modulate(s, r):
                dve.wait_ge(xT_ps, 4 * s + r + 1)
                if r == 0 and s > 0:
                    dve.wait_ge(hl_ready, 4 * s)
                for k in range(2):
                    n = 2 * r + k
                    ins = dve.tensor_scalar(h32[:, n, :], side[(r + 1) % 2][:, k * S:(k + 1) * S],
                                            mcols[:, 0, n:n + 1], mcols[:, 1, n:n + 1], ALU.mult, ALU.add)
                ins.then_inc(h32_ready, 1)

            for q in range(API):
                ada_pair(0, 0, q)
            dve.wait_ge(xroot_ready, 1)
            dve.reciprocal(st[:, ST_R:ST_R + 2], st[:, ST_RT:ST_RT + 2]).then_inc(rstd_ready, 1)
            with dve.Fori(1, NI) as i:
                for q in range(API):
                    ada_pair(0, i, q)
            y, sr, s2, pl = (tl[:, k, :] for k in (1, 2, 3, 4))
            dve.wait_ge(elam_ready, 1)
            link(dve.tensor_scalar(sr, y, 2.0, None, ALU.add))
            link(dve.reciprocal(sr, sr))
            link(dve.tensor_tensor(sr, sr, y, ALU.mult))
            link(dve.tensor_tensor(s2, sr, sr, ALU.mult))
            link(dve.tensor_scalar(pl, s2, 1.0 / 19, None, ALU.mult))
            for k in (17, 15, 13, 11, 9, 7, 5, 3):
                link(dve.scalar_tensor_tensor(out=pl, in0=pl, scalar=1.0 / k, in1=s2, op0=ALU.add, op1=ALU.mult))
            link(dve.scalar_tensor_tensor(out=pl, in0=pl, scalar=1.0, in1=sr, op0=ALU.add, op1=ALU.mult))
            link(dve.tensor_scalar(s2, lam, -1.0, 0.0, ALU.mult, ALU.max))
            link(dve.scalar_tensor_tensor(out=pl, in0=pl, scalar=2.0, in1=s2, op0=ALU.mult, op1=ALU.add))
            dve.tensor_scalar(coef[:], pl, C_RG / 2, None, ALU.mult).then_inc(coef_ready, 1)
            mod_columns(0)
            for r in range(4):
                modulate(0, r)

            def step(s, i, first, last):
                for u in range(TPI):
                    for g in range(GPT):
                        n = u * GPT + g
                        if first and n < 3:
                            for k in ((0, 1), (2,), (3,))[n]:
                                split_h(s, k)
                        if g % 2 == 0 and 2 * u + g // 2 < API:
                            ada_pair(s + 1, i, 2 * u + g // 2)
                        if last and n == TPI * GPT - 2:
                            mod_columns(s + 1)
                            modulate(s + 1, 0)
                            modulate(s + 1, 1)
                        c0 = s * NT * 2 + n // 2
                        split_lo(i * (TPI * GPT) + (s * GSB + n), c0 % NW, n % 2, n % NG)
                    if last and u == TPI - 1:
                        modulate(s + 1, 2)
                        modulate(s + 1, 3)
                    if first and u == 0:
                        if s == 0:
                            dve.wait_ge(rstd_ready, 1)
                            dve.wait_ge(mask_stored, 16)
                        else:
                            evac(s - 1, NT - 1, NT - 1, (NT - 1) % 3)
                    else:
                        evac(s, i * TPI + (u - 1), i * TPI + (u - 1), (u - 1) % 3)

            for s in range(NSB - 1):
                step(s, 0, True, False)
                with dve.Fori(1, NI - 1) as i:
                    step(s, i, False, False)
                step(s, NI - 1, False, True)

            def add_bias(h):
                dve.wait_ge(s_ps, h + 1)
                dve.wait_ge(bias_landed[h % 2], 16 * ROWS * (h // 2 + 1))
                if h >= 2:
                    dve.wait_ge(pT_ps, h - 1)
                dve.scalar_tensor_tensor(out=prob[:, h % 2, :, :], in0=side[3][:].rearrange("p (t n) -> p t n", t=TOK),
                                         scalar=SCALE, in1=bias[:, h % 2, :, :], op0=ALU.mult, op1=ALU.add).then_inc(s_ready, 1)
                dve.wait_ge(s_ready, 2 * h + 1)
                link(dve.tensor_reduce(mx[:, h % 2, :], prob[:, h % 2, :, :], AX, ALU.max))
                dve.tensor_scalar(mx[:, h % 2, :], mx[:, h % 2, :], -1.0, None, ALU.mult).then_inc(s_ready, 1)

            def rinv(h):
                dve.wait_ge(p_ready, 2 * h + 2)
                dve.reciprocal(es[:, h % 4, :], es[:, h % 4, :]).then_inc(rinv_ready, 1)

            def gate_z(t):
                dve.wait_ge(sig_ready, t + 1)
                link(dve.tensor_tensor(sig[:], sig[:], proj[:, GB + t, :, :], ALU.mult))
                dve.tensor_tensor(proj[:, GB + t, :, :], sig[:], proj[:, QB + t, :, :], ALU.mult).then_inc(z_ready, 1)

            def yB_lower(r):
                dve.wait_ge(yB_hi_r, r + 1)
                for k in range(2):
                    n = 2 * r + k
                    ins = dve.scalar_tensor_tensor(out=yB_lo[:, n, :], in0=side[2 + r % 2][:, k * S:(k + 1) * S],
                                                   scalar=par[:, C_GNA + n:C_GNA + n + 1],
                                                   in1=yB_hi[:, n, :].bitcast(F32), op0=ALU.mult, op1=ALU.subtract)
                ins.then_inc(yB_lo_r, 1)

            s = NSB - 1
            for g in range(GSB):
                t = g // GPT
                if g < 3:
                    for k in ((0, 1), (2,), (3,))[g]:
                        split_h(s, k)
                if g % 2 == 0 and g // 2 < APS:
                    q = g // 2
                    for jj in range(2):
                        if q == 0 and jj == 0:
                            dve.wait_ge(gbias_landed, 16)
                        j = q // 2 * 2 + jj
                        ada(NSB * APS * 2 + 2 * q + jj, q % NA, 1, mod, q % 2, jj, cond[:, j:j + 1], False,
                            ((NSB * APS + q) // NA + 1) * 16)
                for h in range(NH):
                    if g == add_bias_at(h):
                        add_bias(h)
                    if g == rinv_at(h):
                        rinv(h)
                if GATE_AT <= g < GATE_AT + 4:
                    gate_z(g - GATE_AT)
                for r in range(NH // 2):
                    if g == yBT_AT + r + 1:
                        yB_lower(r)
                c0 = s * NT * 2 + g // 2
                split_lo(s * GSB + g, c0 % NW, g % 2, g % NG)
                if g % GPT == GPT - 1:
                    if t == 0:
                        evac(s - 1, NT - 1, NT - 1, (NT - 1) % 3)
                    else:
                        evac(s, t - 1, LAST[t - 1], (t - 1) % 2)

            def convolve(g):
                dve.wait_ge(xaT_ready, g // 2 + 1)
                if g >= 1:
                    dve.wait_ge(sq_used, 2 * g)
                for j in range(CONV_W):
                    for k in range(2):
                        b, n = 2 * g + k, C_CW + j * NB + 2 * g + k
                        src = xaT[:, b % 4, j:j + S]
                        if j == 0:
                            ins = dve.tensor_scalar(xc[:, k, :], src, par[:, n:n + 1], par[:, C_CB + b:C_CB + b + 1],
                                                    ALU.mult, ALU.add)
                        else:
                            ins = dve.scalar_tensor_tensor(out=xc[:, k, :], in0=src, scalar=par[:, n:n + 1],
                                                           in1=xc[:, k, :], op0=ALU.mult, op1=ALU.add)
                    if j < CONV_W - 1:
                        link(ins)
                ins.then_inc(xc_ready, 1)

            def gate_silu(q):
                dve.wait_ge(gsig_ready, q + 1)
                for b in range(2):
                    ins = dve.tensor_tensor(gaS[:, 2 * b:2 * b + 2, :], gaS[:, 2 * b:2 * b + 2, :],
                                            side[2 + b][:].rearrange("p (k n) -> p k n", k=2), ALU.mult)
                ins.then_inc(gaS_ready, 1)

            def decay(g):
                dve.wait_ge(v_ready, g + 1)
                dve.tensor_scalar(wa_[:], rv[:], 1.0, None, ALU.add).then_inc(w_ready, 1)
                dve.wait_ge(w_ready, 2 * g + 1)
                dve.reciprocal(wa_[:], wa_[:]).then_inc(w_ready, 1)
                dve.wait_ge(w_ready, 2 * g + 2)
                dve.wait_ge(sq_used, 2 * g + 2)
                link(dve.scalar_tensor_tensor(out=ib[:].rearrange("p e k n -> p (e k n)"), in0=ib[:].rearrange("p e k n -> p (e k n)"),
                                              scalar=2.0, in1=wa_[:].rearrange("p e k n -> p (e k n)"), op0=ALU.mult, op1=ALU.mult))
                dve.wait_ge(sq_ready, g + 1)
                link(dve.tensor_tensor(ib[:], ib[:], rv[:], ALU.mult))
                link(dve.tensor_scalar(wa_[:], wa_[:], 2.0, -1.0, ALU.mult, ALU.add))

            def scans(g):
                if g >= 1:
                    dve.wait_ge(yA_lo_r, g)
                    dve.wait_ge(hsq_ready, g)
                for k in range(2):
                    dve.tensor_tensor_scan(hh[:, 0, k, :], wa_[:, 0, k, :], ib[:, 0, k, :], 0.0, ALU.mult, ALU.add).then_inc(scan_ready, 1)
                    dve.tensor_tensor_scan(hh[:, 1, k, ::-1], wa_[:, 1, k, ::-1], ib[:, 1, k, ::-1], 0.0,
                                           ALU.mult, ALU.add).then_inc(scan_ready, 1)
                dve.wait_ge(scan_ready, 4 * g + 4)
                dve.tensor_tensor(hh[:, 0, :, :], hh[:, 0, :, :], hh[:, 1, :, :], ALU.add).then_inc(h_ready, 1)
                dve.wait_ge(h_ready, g + 1)
                dve.wait_ge(gaS_ready, g // 2 + 1)
                for k in range(2):
                    b = 2 * g + k
                    ins = dve.scalar_tensor_tensor(out=hh[:, 1, k, :], in0=hh[:, 0, k, :],
                                                   scalar=par[:, C_GNL + b:C_GNL + b + 1], in1=gaS[:, b % 4, :],
                                                   op0=ALU.mult, op1=ALU.mult)
                ins.then_inc(y_ready, 1)

            def yA_lower(g):
                dve.wait_ge(yA_hi_r, g + 1)
                dve.tensor_tensor(yA_lo[:, 2 * g:2 * g + 2, :], hh[:, 1, :, :],
                                  yA_hi[:, 2 * g:2 * g + 2, :].bitcast(F32), ALU.subtract).then_inc(yA_lo_r, 1)

            def evac_out(o):
                n = NSB * GSB + (o + 1) * GPO
                dve.wait_ge(gran_used, n)
                t = out_tile(o % NCO)
                if o == 0:
                    dve.wait_ge(rB_ready, 1)
                    link(dve.reciprocal(st[:, ST_BR:ST_BR + 2], st[:, ST_BR:ST_BR + 2]))
                if o == NCO:
                    dve.wait_ge(rA_ready, 1)
                    link(dve.reciprocal(st[:, ST_AR:ST_AR + 2], st[:, ST_AR:ST_AR + 2]))
                if o >= NCO:
                    dve.wait_ge(evac_done, NSB * NT + o - NCO + 1)
                for tok in range(TOK):
                    if o < NCO:
                        ins = dve.tensor_scalar(t[:, tok, :], acc[o % 2][tok][:], st[:, ST_BR + tok:ST_BR + tok + 1], None, ALU.mult)
                    else:
                        ins = dve.scalar_tensor_tensor(out=t[:, tok, :], in0=acc[o % 2][tok][:],
                                                       scalar=st[:, ST_AR + tok:ST_AR + tok + 1], in1=t[:, tok, :],
                                                       op0=ALU.mult, op1=ALU.add)
                ins.then_inc(evac_done, 1)

            for g in range(GOUT):
                for q in range(NB // 4):
                    if g == 16 * q + 6:
                        gate_silu(q)
                for n in range(NB // 2):
                    if g == 8 * n + 4:
                        convolve(n)
                    if g == 8 * n + 11:
                        decay(n)
                    if g == 8 * n + 12:
                        scans(n)
                    if g == 8 * n + 13:
                        yA_lower(n)
                split_lo(NSB * GSB + g, (NSB * NT * 2 + g // 2) % NW, g % 2, g % NG)
                if g % 2 == 0:
                    for q in gate_chunk_at(g // 2):
                        for jj in range(2):
                            if q == 0 and jj == 0:
                                dve.wait_ge(gbias_landed, 32)
                            cn = (NSB + 1) * APS + q
                            j = q % (APS // 2) * 2 + jj
                            ada(cn * 2 + jj, cn % NA, 0, mod2, q // (APS // 2), jj, cond[:, j:j + 1], False, (cn // NA + 1) * 16)
                if g == GPT - 1:
                    evac(NSB - 1, NT - 1, LAST[NT - 1], (NT - 1) % 2)
                for o in range(2 * NCO - 1):
                    if g == evac_at(o):
                        evac_out(o)
            evac_out(2 * NCO - 1)
            dve.wait_ge(fss_ready, 2 * NCO)
            dve.tensor_reduce(st[:, ST_F:ST_F + 2], fss[:], AX, ALU.add).then_inc(fsum_ready, 1)
            dve.wait_ge(rF_ready, 1)
            link(dve.reciprocal(st[:, ST_FR:ST_FR + 2], st[:, ST_FR:ST_FR + 2]))
            for t in range(NCO):
                dve.wait_ge(t4_ready, t + 1)
                for tok in range(TOK):
                    ins = dve.tensor_scalar(out_tile(t)[:, tok, :], out_tile(t)[:, tok, :],
                                            st[:, ST_FR + tok:ST_FR + tok + 1], None, ALU.mult)
                ins.then_inc(fin_ready, 1)

        @block.tensor
        def _(pe):
            pe.wait_ge(consts_ready, 2)
            pe.wait_ge(par_landed, 16 * 10)
            pe.transpose(side[0][:, 0:P], par_rows[:, 0, :], ident[:])
            pe.transpose(side[0][:, P:2 * P], par_rows[:, 1, :], ident[:])
            pe.transpose(side[0][:, 2 * P:NPAR], par_rows[0:NPAR - 2 * P, 2, :],
                         ident[0:NPAR - 2 * P, 0:NPAR - 2 * P]).then_inc(par_ps, 1)

            def granule(slot, up, low, k0, buf, first, last, gr):
                pe.wait_ge(lo_ready, gr + 1)
                for k in range(GK):
                    for tok in range(TOK):
                        lh = up[:, k0 + k, tok * P:(tok + 1) * P]
                        ll = low[:, k0 + k, tok * P:(tok + 1) * P]
                        pe.matmul(acc[buf][tok][:], lh, w_hi[:, slot, k, :], start=first and k == 0, stop=False)
                        pe.matmul(acc[buf][tok][:], lh, w_lo[:, slot, k, :], start=False, stop=False)
                        ins = pe.matmul(acc[buf][tok][:], ll, w_hi[:, slot, k, :], start=False, stop=last and k == GK - 1)
                ins.then_inc(gran_used, 1)

            def mod_sums(s):
                pe.wait_ge(ada_step, 2 * APS * (s + 1))
                if s == 0:
                    pe.wait_ge(par_ready, 1)
                else:
                    pe.wait_ge(h32_ready, 4 * s)
                for k in range(2 * KT):
                    ins = pe.matmul(side[0][:, k:k + 1], mod[:, k // KT, (k % KT) * P:(k % KT + 1) * P], ones[:, 0:1],
                                    start=True, stop=True)
                ins.then_inc(mod_ps, 1)

            def transpose_x(s, r):
                pe.wait_ge(xs_scaled, 2 * (s + 1))
                if r == 1:
                    pe.wait_ge(mod_cols, 2 * s + 2)
                if r >= 2:
                    pe.wait_ge(h32_ready, 4 * s + r - 1)
                for k in range(2):
                    for tok in range(TOK):
                        ins = pe.transpose(side[(r + 1) % 2][:, k * S + tok * P:k * S + (tok + 1) * P],
                                           xs[:, tok, (2 * r + k) * P:(2 * r + k + 1) * P], ident[:])
                ins.then_inc(xT_ps, 1)

            mod_sums(0)
            for r in range(4):
                transpose_x(0, r)

            def step(s, i, first, last):
                for u in range(TPI):
                    n = i * TPI + (s * NT + u)
                    if not (isinstance(n, int) and n < 3):
                        pe.wait_ge(evac_done, n - 2)
                    for g in range(GPT):
                        if first and u == 0:
                            pe.wait_ge(hl_ready, 4 * s + g + 1)
                        gr = i * (TPI * GPT) + (s * GSB + u * GPT + g)
                        granule((u * GPT + g) % NG, h_hi, h_lo, GK * g, u, g == 0, g == GPT - 1, gr)
                        if last and u == TPI - 2 and g == GPT - 1:
                            mod_sums(s + 1)
                            transpose_x(s + 1, 0)
                        if last and u == TPI - 1 and g < 3:
                            transpose_x(s + 1, g + 1)

            for s in range(NSB - 1):
                step(s, 0, True, False)
                with pe.Fori(1, NI - 1) as i:
                    step(s, i, False, False)
                step(s, NI - 1, False, True)

            def transpose_qk(h):
                if h == 0:
                    pe.wait_ge(hl_ready, 4 * NSB)
                tile = 3 * (h // 4) + 2
                pe.wait_ge(evac_done, (NSB - 1) * NT + tile + 1)
                if h >= 1:
                    pe.wait_ge(qkT_ready, h)
                for a, part in enumerate((QB, KB)):
                    for tok in range(TOK):
                        ins = pe.transpose(side[2][:, a * S + tok * P:a * S + (tok + 1) * P], head(part, h, tok), ident[:])
                ins.then_inc(qkT_ps, 1)

            def scores(h):
                pe.wait_ge(qkT_ready, h + 1)
                if h >= 1:
                    pe.wait_ge(s_ready, 2 * h - 1)
                for tok in range(TOK):
                    ins = pe.matmul(side[3][:, tok * S:(tok + 1) * S], qkT[:, 0, tok * P:(tok + 1) * P], qkT[:, 1, :],
                                    start=True, stop=True)
                ins.then_inc(s_ps, 1)

            def transpose_p(h):
                pe.wait_ge(p_ready, 2 * h + 2)
                if h >= 1:
                    pe.wait_ge(pT_ready, h)
                for kt in range(2):
                    for tok in range(TOK):
                        ins = pe.transpose(side[0][:, kt * S + tok * P:kt * S + (tok + 1) * P],
                                           prob[:, h % 2, tok, kt * P:(kt + 1) * P], ident[:])
                ins.then_inc(pT_ps, 1)

            def p_times_v(h):
                pe.wait_ge(pT_ready, h + 1)
                if h >= 1:
                    pe.wait_ge(o_ready, h)
                for tok in range(TOK):
                    for kt in range(2):
                        ins = pe.matmul(side[1][:, tok * P:(tok + 1) * P], probT[:, kt, tok * P:(tok + 1) * P],
                                        head(VB, h, kt), start=(kt == 0), stop=(kt == 1))
                ins.then_inc(o_ps, 1)

            def transpose_yB(r):
                pe.wait_ge(z_ready, r // 2 + 1)
                if r == 0:
                    pe.wait_ge(s_ready, 2 * NH)
                if r >= 2:
                    pe.wait_ge(yB_lo_r, r - 1)
                for k in range(2):
                    for tok in range(TOK):
                        ins = pe.transpose(side[2 + r % 2][:, k * S + tok * P:k * S + (tok + 1) * P],
                                           head(GB, 2 * r + k, tok), ident[:])
                ins.then_inc(yBT_ps, 1)

            s = NSB - 1
            for g in range(GSB):
                t = g // GPT
                for h in range(NH):
                    if g == qk_at(h):
                        transpose_qk(h)
                    if g == scores_at(h):
                        scores(h)
                    if g == pT_at(h):
                        transpose_p(h)
                    if g == pv_at(h):
                        p_times_v(h)
                for r in range(NH // 2):
                    if g == yBT_AT + r - 2:
                        transpose_yB(r)
                if g % GPT == 0:
                    pe.wait_ge(evac_done, s * NT + t - 1)
                if g < GPT:
                    pe.wait_ge(hl_ready, 4 * s + g + 1)
                granule(g % NG, h_hi, h_lo, GK * (g % GPT), t % 2, g % GPT == 0, g % GPT == GPT - 1, s * GSB + g)

            def transpose_lru(q, part, bank, done):
                if part == XB:
                    if q == 0:
                        pe.wait_ge(evac_done, (NSB - 1) * NT + NT - 1)
                        pe.wait_ge(o_ready, NH)
                    else:
                        pe.wait_ge(ri_ready, 2 * q)
                elif q == 0:
                    pe.wait_ge(yB_lo_r, NH // 2)
                for k in range(4):
                    for tok in range(TOK):
                        ins = pe.transpose(side[bank + k // 2][:, (k % 2) * S + tok * P:(k % 2) * S + (tok + 1) * P],
                                           proj[:, part + q, tok, k * P:(k + 1) * P], ident[:])
                ins.then_inc(done, 1)

            def lru_gates(g):
                pe.wait_ge(xc_ready, g + 1)
                pe.wait_ge(gwt_landed, 64 * (g + 1))
                pe.wait_ge(gaS_ready, g // 2 + 1)
                if g >= 1:
                    pe.wait_ge(ri_ready, g)
                for e in range(2):
                    for k in range(2):
                        for n in range(2):
                            ins = pe.matmul(side[2 * e + k][:, n * S:(n + 1) * S], gate_wt[:, k, e, n, :], xc[:, n, :],
                                            start=True, stop=True)
                ins.then_inc(gate_ps, 1)

            def sum_squares_A():
                pe.wait_ge(hacc_ready, NB // 2)
                pe.wait_ge(ri_ready, NB // 2)
                for tok in range(TOK):
                    for k in range(2):
                        ins = pe.matmul(side[0][:, tok:tok + 1], hacc[:, k, tok * P:(tok + 1) * P], ones[:, 0:1],
                                        start=(k == 0), stop=(k == 1))
                ins.then_inc(ssA_ps, 1)

            def gate_broadcast(n):
                if n == 0:
                    pe.wait_ge(ada_step, 2 * (NSB + 1) * APS)
                    pe.wait_ge(ri_ready, NB // 2)
                if n == 4:
                    pe.wait_ge(ada_step, 2 * (NSB + 1) * APS + APS)
                if n == 6:
                    pe.wait_ge(ada_step, 2 * (NSB + 2) * APS)
                if n >= 3:
                    pe.wait_ge(gate_ready, n - 2)
                m = mod if n < 4 else mod2
                pe.matmul(side[1 + n % 3][:], ones[:], m[:, (n % 4) // 2, (n % 2) * CT:(n % 2 + 1) * CT],
                          start=True, stop=True).then_inc(gate_bc_ps, 1)

            for g in range(GOUT):
                for q in range(NB // 4):
                    if g == 16 * q:
                        transpose_lru(q, XB, 0, xaT_ps)
                    if g == 16 * q + 1:
                        transpose_lru(q, GA, 2, gaT_ps)
                for n in range(NB // 2):
                    if g == 8 * n + 6:
                        lru_gates(n)
                if g == NORM_A_AT:
                    sum_squares_A()
                for n in range(NCO):
                    if g == gate_bc_at(n):
                        gate_broadcast(n)
                o, k = g // GPO, g % GPO
                if k == 0:
                    pe.wait_ge(evac_done, NSB * NT + o - 1)
                if o == 0:
                    pe.wait_ge(yB_lo_r, k + 1)
                if o == NCO:
                    pe.wait_ge(yA_lo_r, k + 1)
                up, low = (yB_hi, yB_lo) if o < NCO else (yA_hi, yA_lo)
                granule(g % NG, up, low, GK * k, o % 2, k == 0, k == GPO - 1, NSB * GSB + g)


def qk_at(h): return 3 * h + 17
def copy_qkT_at(h): return qk_at(h) + 3
def scores_at(h): return qk_at(h) + 5
def add_bias_at(h): return scores_at(h) + 3
def exps_at(h): return add_bias_at(h) + 1
def pT_at(h): return exps_at(h) + 2
def copy_probT_at(h): return pT_at(h) + 3
def pv_at(h): return copy_probT_at(h) + 1
def rinv_at(h): return pv_at(h) + 1
def scale_o_at(h): return pv_at(h) + 3


GATE_AT = scale_o_at(NH - 1) + 1
NORM_B_AT = GATE_AT + 4
yBT_AT = GATE_AT + 5
NORM_A_AT = NCO * GPO + 8


def evac_at(o): return (o + 1) * GPO + 3
def gate_bc_at(n): return NCO * GPO + (10 + n if n < 4 else 40 + (n - 4) if n < 6 else 59 + (n - 6))


def gate_chunk_at(n):
    k = n - (NCO * GPO // WCH + 3)
    if k < 0 or k >= 2 * 16 - 6:
        return []
    lead = [1] * 6 + [2] * 6 + [1] * 14
    at = sum(lead[:k])
    return list(range(at, min(at + lead[k], APS))) if k < len(lead) else []


_OUT = ((1, S, D), 'float32')
_NAMES = ['x', 'c', 'norm_g', 'w_ada', 'b_ada', 'w_in', 'conv_w', 'conv_b', 'lru_wa', 'lru_ba', 'lru_wx', 'lru_bx',
          'lru_lambda', 'rpb', 'gn_lru', 'gn_att', 'w_out', 'final_g']


def kernel(**inputs):
    import numpy as np
    import concourse.bacc as bacc
    from concourse.bass_utils import run_bass_kernel_spmd

    nc = bacc.Bacc("TRN2", target_bir_lowering=False, num_devices=1)
    arrays, args = {}, []
    for name in _NAMES:
        a = np.ascontiguousarray(inputs[name])
        arrays[f"in_{name}"] = a
        args.append(nc.dram_tensor(f"in_{name}", a.shape, mybir.dt.from_np(a.dtype), kind="ExternalInput").ap())
    out = nc.dram_tensor("out_0", _OUT[0], F32, kind="ExternalOutput").ap()
    build(nc, *args, out)
    r = run_bass_kernel_spmd(nc, [arrays], core_ids=[0])
    return r.results[0]["out_0"]
```

```python
from concourse import mybir
import concourse.bass as bass

ALU = mybir.AluOpType
ACT = mybir.ActivationFunctionType
AX = mybir.AxisListType.X
F32 = mybir.dt.float32
F32R = mybir.dt.float32r

P = 128
D = 4096
S = 256
TOK = S // P
W = 2048
D_IN = 6 * W
NB = 16
CONV_W = 4
C_RG = 8.0
NH = 16
GW = 64
ROWS = S // GW
WIN_R, WIN_C = 8, 16
NRO = 2 * ROWS - 1
RPB_W = 2 * WIN_C - 1
RO0 = WIN_R - ROWS
EPS = 1e-6
MASK = -1e30
SCALE = float(P) ** -0.5

NSB = 4
KT = D // P // NSB
SBW = KT * P
CT = 512
NT = D_IN // CT
GK = 2
GPT = KT // GK
WCH = 2
NW = 3
NG = 3
NA = 4
TPI = 3
NI = NT // TPI
API = 8
APS = NI * API
GSB = NT * GPT
NCO = D // CT
GPO = W // P // GK
GOUT = 2 * NCO * GPO
QB, KB, VB, GB, XB, GA = 8, 12, 16, 20, 0, 4
LAST = [QB, KB, VB, QB + 1, KB + 1, VB + 1, QB + 2, KB + 2, VB + 2, QB + 3, KB + 3, VB + 3,
        GB, GB + 1, GB + 2, GB + 3, 0, 1, 2, 3, GA, GA + 1, GA + 2, GA + 3]

C_C, C_NG, C_BSH, C_BSC = 0, 32, 64, 96
C_CW, C_CB, C_GNL, C_BA = 128, 192, 208, 224
C_BX, C_LAM, C_GNA = 256, 288, 320
NPAR = 336


def build(nc, x, c, norm_g, w_ada, b_ada, w_in, conv_w, conv_b, lru_wa, lru_ba, lru_wx, lru_bx,
          lru_lambda, rpb, gn_lru, gn_att, w_out, final_g, out):
    top = [(nc.sbuf_base + 31) // 32 * 32]

    def region(size):
        at = top[0]
        top[0] += (size + 31) // 32 * 32
        assert top[0] <= nc.sbuf_usable_end, top[0]
        return at

    def place(name, shape, at, dt=F32):
        return nc.alloc_sbuf_tensor_at(name, [P] + shape, dt, offset=at)

    def sem(name):
        return nc.alloc_semaphore(name)

    TB = TOK * CT * 4
    at_p = region(NT * TB)
    at_h = region(2 * KT * S * 4)
    at_h32 = region(KT * S * 4 + 32)
    at_xs = region(TOK * SBW * 4)
    at_mod = region(2 * SBW * 4)
    at_wst = region(NW * WCH * GK * CT * 4)
    at_ast = region(NA * SBW * 4)
    at_whi = region(NG * GK * CT * 4)
    at_wlo = region(NG * GK * CT * 4)

    proj = place("proj", [NT, TOK, CT], at_p)
    h_hi = place("h_hi", [KT, S], at_h, F32R)
    h_lo = place("h_lo", [KT, S], at_h + KT * S * 4, F32R)
    xs = place("xs", [TOK, SBW], at_xs)
    h32 = place("h32", [KT, S], at_h32)
    mod = place("mod", [2, SBW], at_mod)
    w_st = place("w_st", [NW, WCH, GK, CT], at_wst)
    a_st = place("a_st", [NA, SBW], at_ast)
    w_hi = place("w_hi", [NG, GK, CT], at_whi, F32R)
    w_lo = place("w_lo", [NG, GK, CT], at_wlo, F32R)
    xfull = place("xfull", [TOK, D], at_p)
    maskfill = place("maskfill", [GW * NH * NRO * GW // P], at_p + GB * TB)
    qkT = place("qkT", [2, S], at_xs)
    prob = place("prob", [2, TOK, S], at_xs + 2048)
    probT = place("probT", [2, S], at_xs + 6144)
    bias = place("bias", [2, TOK, S], at_h32)
    sig = place("sig", [TOK, CT], at_h32 + 4096)
    yB_hi = place("yB_hi", [NH, S], at_p + KB * TB, F32R)
    yB_lo = place("yB_lo", [NH, S], at_p + VB * TB, F32R)
    yA_hi = place("yA_hi", [NB, S], at_p + GA * TB, F32R)
    yA_lo = place("yA_lo", [NB, S], at_p + XB * TB, F32R)
    yA = place("yA", [NB, S], at_p + XB * TB)
    XPAD = S + 4
    xaT = place("xaT", [2, XPAD], at_h)
    gaS = place("gaS", [2, S], at_h + 2080)
    xc = place("xc", [2, 2, S], at_h + 4128)
    hsq = place("hsq", [2, S], at_h + 8224)
    hacc = place("hacc", [2, S], at_h + 10272)
    rv = place("rv", [2, 2, S], at_h + 12320)
    ib = place("ib", [2, 2, S], at_h + 16416)
    wa_ = place("wa_", [2, 2, S], at_h + 20512)
    fing = place("fing", [D], at_h)
    xres = place("xres", [2, TOK, CT], at_h32)
    mod2 = place("mod2", [2, SBW], at_xs)
    at_gw = region(4096)
    gate_wt = [place("gate_wt0", [2, 2, 2, P], at_gw), place("gate_wt1", [2, 2, 2, P], at_p + (GB + 3) * TB)]
    ident = place("ident", [P], region(512))
    ones = place("ones", [P], region(512))
    par_rows = place("par_rows", [3, P], at_gw)
    par = place("par", [NPAR], region(NPAR * 4))
    cond = place("cond", [32], region(128))
    mcols = place("mcols", [3, KT], region(96))
    coef = place("coef", [2, 32], region(256))
    tl = place("tl", [5, 32], region(640))
    st = place("st", [64], region(256))
    fss = place("fss", [TOK, NCO], region(64))
    mx = place("mx", [2, TOK], region(32))
    es = place("es", [4, TOK], region(32))
    ST_SS, ST_RT, ST_R, ST_EPS, ST_B, ST_BR, ST_A, ST_AR, ST_F, ST_FR = 0, 2, 4, 6, 8, 10, 12, 14, 16, 18

    banks = [nc.alloc_psum_tensor(f"bank{i}", [P, 512], F32) for i in range(8)]
    acc = [banks[0:2], banks[2:4], banks[4:6]]
    side = [banks[6], banks[7], banks[4], banks[5]]

    bias_img = nc.dram_tensor("bias_img", (GW, NH, NRO, GW), F32, kind="Internal").ap()

    w_landed = [sem(f"w_landed{i}") for i in range(NW)]
    a_landed = [sem(f"a_landed{i}") for i in range(NA)]
    hi_ready, lo_ready, gran_used = sem("hi_ready"), sem("lo_ready"), sem("gran_used")
    evac_done, ada_step = sem("evac_done"), sem("ada_step")
    mod_ps, mod_cols, xs_landed, xs_scaled = sem("mod_ps"), sem("mod_cols"), sem("xs_landed"), sem("xs_scaled")
    xT_ps, h32_ready, hh_ready, hl_ready = sem("xT_ps"), sem("h32_ready"), sem("hh_ready"), sem("hl_ready")
    par_landed, par_ps, par_ready, cond_ready = sem("par_landed"), sem("par_ps"), sem("par_ready"), sem("cond_ready")
    consts_ready, x_landed, rstd_ready = sem("consts_ready"), sem("x_landed"), sem("rstd_ready")
    coef_ready, eps_ready = sem("coef_ready"), sem("eps_ready")
    mask_set, mask_stored, img_stored = sem("mask_set"), sem("mask_stored"), sem("img_stored")
    bias_landed = [sem("bias_landed0"), sem("bias_landed1")]
    qkT_ps, qkT_ready, s_ps, s_ready = sem("qkT_ps"), sem("qkT_ready"), sem("s_ps"), sem("s_ready")
    p_ready, pT_ps, pT_ready, o_ps, o_ready = sem("p_ready"), sem("pT_ps"), sem("pT_ready"), sem("o_ps"), sem("o_ready")
    rinv_ready = sem("rinv_ready")
    sig_ready, z_ready, yBT_ps, yB_hi_r, yB_lo_r = sem("sig_ready"), sem("z_ready"), sem("yBT_ps"), sem("yB_hi_r"), sem("yB_lo_r")
    rB_ready, rA_ready = sem("rB_ready"), sem("rA_ready")
    xaT_ps, gaT_ps, xaT_ready, gsig_ready, gaS_ready = sem("xaT_ps"), sem("gaT_ps"), sem("xaT_ready"), sem("gsig_ready"), sem("gaS_ready")
    pad_set, xc_ready, gate_ps, ri_ready, v_ready = sem("pad_set"), sem("xc_ready"), sem("gate_ps"), sem("ri_ready"), sem("v_ready")
    gwt_landed = [sem("gwt_landed0"), sem("gwt_landed1")]
    r_ready, m_ready, b_ready, sq_ready, scan_ready, h_ready, y_ready = sem("r_ready"), sem("m_ready"), sem("b_ready"), sem("sq_ready"), sem("scan_ready"), sem("h_ready"), sem("y_ready")
    a_ready, yA_hi_r, yA_lo_r, hacc_ready, ssA_ps = sem("a_ready"), sem("yA_hi_r"), sem("yA_lo_r"), sem("hacc_ready"), sem("ssA_ps")
    hsq_ready = sem("hsq_ready")
    gzero, gbias_landed, gate_bc_ps, gate_ready = sem("gzero"), sem("gbias_landed"), sem("gate_bc_ps"), sem("gate_ready")
    fing_landed, ixc_ready = sem("fing_landed"), sem("ixc_ready")
    xres_landed = [sem("xres_landed0"), sem("xres_landed1")]
    t3_ready, fss_ready, t4_ready, rF_ready, fin_ready, out_stored = (
        sem("t3_ready"), sem("fss_ready"), sem("t4_ready"), sem("rF_ready"), sem("fin_ready"), sem("out_stored"))
    sigc_ready, xroot_ready, lam_ready, elam_ready, fsum_ready = (
        sem("sigc_ready"), sem("xroot_ready"), sem("lam_ready"), sem("elam_ready"), sem("fsum_ready"))
    dve_step, act_step, pool_step = sem("dve_step"), sem("act_step"), sem("pool_step")

    x_v = x.rearrange("b (t p) d -> p (b t) d", p=P)
    out_v = out.rearrange("b (t p) d -> p (b t) d", p=P)
    w_in_v = w_in.rearrange("l (k p) n -> p (l k) n", p=P)
    w_ada_v = w_ada.rearrange("l (k p) n -> p (l k) n", p=P)
    w_out_v = w_out.rearrange("l (k p) n -> p (l k) n", p=P)
    b_gate = b_ada[:, 2 * D:3 * D]

    def gran_of_tile(t):
        return GPT * t

    def chunk_wait(eng, wc_slot, n):
        eng.wait_ge(w_landed[wc_slot], n)

    def proj_at(t, tok=None):
        if isinstance(t, int):
            v = proj[:, t, :, :]
        else:
            v = proj[:, bass.ds(t, 1), :, :].rearrange("p a t n -> p (a t) n")
        return v if tok is None else v[:, tok, :]

    def head(part, h, tok):
        return proj[:, part + h // 4, tok, (h % 4) * P:(h % 4 + 1) * P]

    def out_tile(o):
        return proj[:, (QB + o) if o < 4 else (GB + o - 4), :, :]

    block = nc.Block()
    with block:
        @block.sync
        def _(sp):
            def w_in_chunk(s, i, tile_col, u, half):
                base = s * NT * 2 + 2 * u + half
                n = i * (2 * TPI) + base
                k0 = s * KT + half * WCH * GK
                src = w_in_v[:, k0:k0 + WCH * GK, bass.ds(tile_col * CT, CT)]
                if not (isinstance(n, int) and n < NW):
                    sp.wait_ge(lo_ready, n * 2 - 4)
                sp.dma_start(w_st[:, base % NW, :, :, :].rearrange("p a b n -> p (a b) n"), src).then_inc(w_landed[base % NW], 16)

            def ada_dma(n0, i, q, col0):
                n = i * API + (n0 + q)
                j = i * (API // 2) + q // 2
                src = w_ada_v[:, bass.ds(j, 1), col0:col0 + SBW].rearrange("p a n -> p (a n)")
                if not (isinstance(n, int) and n < NA):
                    sp.wait_ge(ada_step, n - (NA - 1))
                sp.dma_start(a_st[:, q % NA, :], src).then_inc(a_landed[q % NA], 16)

            def ada_col(s, q):
                return (D if q % 2 == 1 else 0) + s * SBW

            for q in range(API):
                ada_dma(0, 0, q, ada_col(0, q))
                if q == NA - 1:
                    for n in range(NW):
                        w_in_chunk(0, 0, n // 2, n // 2, n % 2)
            with sp.Fori(1, NI) as i:
                for q in range(API):
                    ada_dma(0, i, q, ada_col(0, q))

            def step(s, i, last):
                for n in range(2 * TPI):
                    for q in ada_with(n, last):
                        ada_dma((s + 1) * APS, i, q, ada_col(s + 1, q))
                    if not (s == 0 and isinstance(i, int) and i == 0 and n < NW):
                        w_in_chunk(s, i, i * TPI + n // 2, n // 2, n % 2)

            for s in range(NSB - 1):
                step(s, 0, False)
                with sp.Fori(1, NI - 1) as i:
                    step(s, i, False)
                step(s, NI - 1, True)
            s = NSB - 1
            for t in range(NT):
                for half in range(2):
                    n = 2 * t + half
                    if n == 0:
                        sp.wait_ge(gbias_landed, 16)
                    for q in gate1_with(n):
                        ada_dma(NSB * APS, q // API, q % API, 2 * D + (q % 2) * SBW)
                    w_in_chunk(s, t // TPI, LAST[t], t % TPI, half)
            for n in range(GOUT // WCH):
                tile, half = n // (GPO // WCH), n % (GPO // WCH)
                wc = NSB * NT * 2 + n
                sp.wait_ge(lo_ready, wc * 2 - 4)
                k0 = (W // P if tile < NCO else 0) + half * WCH * GK
                sp.dma_start(w_st[:, wc % NW, :, :, :].rearrange("p a b n -> p (a b) n"),
                             w_out_v[:, k0:k0 + WCH * GK, (tile % NCO) * CT:(tile % NCO + 1) * CT]).then_inc(w_landed[wc % NW], 16)
                for g in range(NB // 2):
                    if n == gate_wt_with(g):
                        if g == 1:
                            sp.wait_ge(yB_lo_r, NH // 2)
                        if g >= 2:
                            sp.wait_ge(gate_ps, 2 * (g - 1))
                        for k, w in enumerate((lru_wa, lru_wx)):
                            for e in range(2):
                                sp.dma_start(gate_wt[g % 2][:, k, e, :, :],
                                             w[0, e, 2 * g:2 * g + 2, :, :].rearrange("n k j -> k n j")).then_inc(gwt_landed[g % 2], 16)
                for q in gate2_with(n):
                    cn = (NSB + 1) * APS + q
                    sp.wait_ge(ada_step, cn - (NA - 1))
                    j = q % (APS // 2)
                    col = 2 * D + (2 + q // (APS // 2)) * SBW
                    sp.dma_start(a_st[:, cn % NA, :], w_ada_v[:, j, col:col + SBW]).then_inc(a_landed[cn % NA], 16)
            for t in range(NCO):
                sp.wait_ge(fin_ready, t + 1)
                sp.dma_start(out_v[:, :, t * CT:(t + 1) * CT], out_tile(t)).then_inc(out_stored, 16)
            sp.wait_ge(out_stored, 16 * NCO)

        @block.gpsimd
        def _(pool):
            steps = [0]

            def link(ins):
                steps[0] += 1
                ins.then_inc(pool_step, 1)
                pool.wait_ge(pool_step, steps[0])

            pool.memset(st[:, ST_EPS:ST_EPS + 1], EPS).then_inc(eps_ready, 1)
            link(pool.memset(ident[:], 0.0))
            pool.affine_select(out=ident[:], in_=ident[:], compare_op=ALU.not_equal, fill=1.0, base=0,
                               pattern=[[-1, P]], channel_multiplier=1).then_inc(consts_ready, 1)
            pool.memset(ones[:], 1.0).then_inc(consts_ready, 1)
            pool.dma_start(xfull[:], x_v).then_inc(x_landed, 16)
            pool.dma_start(xs[:], x_v[:, :, 0:SBW]).then_inc(xs_landed, 16)
            pool.memset(maskfill[:], MASK).then_inc(mask_set, 1)
            pool.wait_ge(mask_set, 1)
            pool.dma_start(bias_img.rearrange("c h r k -> (c h r k)").rearrange("(p n) -> p n", p=P),
                           maskfill[:]).then_inc(mask_stored, 16)

            def scale_xs(s):
                pool.wait_ge(xs_landed, 16 * (s + 1))
                pool.wait_ge(rstd_ready, 1)
                for tok in range(TOK):
                    pool.tensor_scalar(xs[:, tok, :], xs[:, tok, :], st[:, ST_R + tok:ST_R + tok + 1], None,
                                       ALU.mult).then_inc(xs_scaled, 1)

            scale_xs(0)
            pool.wait_ge(mask_stored, 16)
            img = bias_img
            HALF = WIN_C // 2
            last_c = GW - WIN_C
            n_store = 0
            for ro in range(NRO):
                tab = rpb[0, :, RO0 + ro, :]
                for c0, nc_, tstep, istep, t0, k0 in (
                    (0, HALF, -1, 0, WIN_C - 1, 0),
                    (HALF, last_c + 1, 0, 1, WIN_C - 1 - HALF, 0),
                    (last_c + HALF + 1, HALF - 1, -1, 0, WIN_C - 1 - HALF - 1, last_c),
                ):
                    src = bass.AP(tensor=tab.tensor, offset=tab.offset + t0,
                                  ap=[[tab.ap[0][0], NH], [tstep, nc_], [1, WIN_C]])
                    at = img[c0, 0, ro, k0:k0 + 1]
                    dst = bass.AP(tensor=img.tensor, offset=at.offset,
                                  ap=[[NRO * GW, NH], [NH * NRO * GW + istep, nc_], [1, WIN_C]])
                    pool.dma_start(dst, src).then_inc(img_stored, 16)
                    n_store += 1
            for s in range(1, NSB):
                pool.wait_ge(xT_ps, 4 * s)
                pool.dma_start(xs[:], x_v[:, :, s * SBW:(s + 1) * SBW]).then_inc(xs_landed, 16)
                scale_xs(s)
            pool.wait_ge(mod_ps, NSB)
            pool.memset(mod[:], 0.0).then_inc(gzero, 1)
            pool.wait_ge(gzero, 1)
            pool.dma_start(mod[0:1, :, :].rearrange("p a n -> p (a n)"), b_gate[:, 0:2 * SBW]).then_inc(gbias_landed, 16)
            pool.wait_ge(img_stored, 16 * n_store)
            pool.wait_ge(hl_ready, 4 * NSB)
            for h in range(NH):
                if h >= 2:
                    pool.wait_ge(s_ready, 2 * (h - 1))
                for r in range(ROWS):
                    pool.dma_start(bias[(r % 2) * GW:(r % 2 + 1) * GW, h % 2, r // 2, :].rearrange("p (a n) -> p a n", a=ROWS),
                                   bias_img[:, h, ROWS - 1 - r:2 * ROWS - 1 - r, :]).then_inc(bias_landed[h % 2], 16)
            pool.wait_ge(gran_used, NSB * GSB)
            pool.memset(xaT[:], 0.0).then_inc(pad_set, 1)
            pool.memset(hacc[:], 0.0).then_inc(pad_set, 1)
            pool.wait_ge(pad_set, 2)
            pool.wait_ge(yB_lo_r, NH // 2)
            pool.memset(mod2[:], 0.0).then_inc(gzero, 1)
            pool.wait_ge(gzero, 2)
            pool.dma_start(mod2[0:1, :, :].rearrange("p a n -> p (a n)"), b_gate[:, 2 * SBW:4 * SBW]).then_inc(gbias_landed, 16)
            for g in range(NB // 2):
                for e in range(2):
                    pool.wait_ge(ri_ready, 2 * g + e + 1)
                    pool.tensor_tensor(ib[:, e, :, :], ib[:, e, :, :], xc[:, g % 2, :, :], ALU.mult).then_inc(ixc_ready, 1)
                pool.wait_ge(h_ready, g + 1)
                pool.tensor_tensor(hsq[:], rv[:, 0, :, :], rv[:, 0, :, :], ALU.mult).then_inc(hsq_ready, 1)
                pool.wait_ge(hsq_ready, g + 1)
                pool.tensor_tensor(hacc[:], hacc[:], hsq[:], ALU.add).then_inc(hacc_ready, 1)
                pool.wait_ge(hacc_ready, g + 1)
            pool.wait_ge(yA_lo_r, NB // 2)
            pool.wait_ge(ssA_ps, 1)
            pool.dma_start(fing[:], final_g.rearrange("(a n) -> a n", a=1).to_broadcast([P, D])).then_inc(fing_landed, 16)
            for t in range(2):
                pool.dma_start(xres[:, t, :, :], x_v[:, :, t * CT:(t + 1) * CT]).then_inc(xres_landed[t], 16)
            for t in range(NCO):
                o = out_tile(t)
                gate = (mod if t < 4 else mod2)[:, (t % 4) // 2, (t % 2) * CT:(t % 2 + 1) * CT]
                pool.wait_ge(evac_done, NSB * NT + NCO + t + 1)
                pool.wait_ge(gate_ready, t + 1)
                for tok in range(TOK):
                    pool.tensor_tensor(o[:, tok, :], o[:, tok, :], gate, ALU.mult).then_inc(pool_step, 1)
                    steps[0] += 1
                pool.wait_ge(pool_step, steps[0])
                pool.wait_ge(xres_landed[t % 2], 16 * (t // 2 + 1))
                pool.tensor_tensor(o, o, xres[:, t % 2, :, :], ALU.add).then_inc(t3_ready, 1)
                if t + 2 < NCO:
                    pool.wait_ge(t3_ready, t + 1)
                    pool.dma_start(xres[:, t % 2, :, :], x_v[:, :, (t + 2) * CT:(t + 3) * CT]).then_inc(xres_landed[t % 2], 16)
                pool.wait_ge(fss_ready, 2 * t + 2)
                if t == 0:
                    pool.wait_ge(fing_landed, 16)
                for tok in range(TOK):
                    ins = pool.tensor_tensor(o[:, tok, :], o[:, tok, :], fing[:, t * CT:(t + 1) * CT], ALU.mult)
                ins.then_inc(t4_ready, 1)

        @block.scalar
        def _(act):
            steps = [0]

            def link(ins):
                steps[0] += 1
                ins.then_inc(act_step, 1)
                act.wait_ge(act_step, steps[0])

            def dma(dst, src):
                act.dma_start(dst, src).then_inc(par_landed, 16)

            r = par_rows
            dma(r[0:32, 0, :], c.rearrange("b (n p) -> (b n) p", p=P))
            dma(r[32:64, 0, :], norm_g.rearrange("l (n p) -> (l n) p", p=P))
            dma(r[64:128, 0, :], b_ada[:, 0:2 * D].rearrange("l (n p) -> (l n) p", p=P))
            dma(r[0:64, 1, :], conv_w.rearrange("l j (n p) -> (l j n) p", p=P))
            dma(r[64:80, 1, :], conv_b.rearrange("l (n p) -> (l n) p", p=P))
            dma(r[80:96, 1, :], gn_lru.rearrange("l (n p) -> (l n) p", p=P))
            dma(r[96:128, 1, :], lru_ba.rearrange("l e (n p) -> (l e n) p", p=P))
            dma(r[0:32, 2, :], lru_bx.rearrange("l e (n p) -> (l e n) p", p=P))
            dma(r[32:64, 2, :], lru_lambda.rearrange("l e (n p) -> (l e n) p", p=P))
            dma(r[64:80, 2, :], gn_att.rearrange("l (n p) -> (l n) p", p=P))
            act.wait_ge(par_ps, 1)
            act.copy(par[:], side[0][:, 0:NPAR]).then_inc(par_ready, 1)
            act.wait_ge(par_ready, 1)
            act.activation(cond[:], par[:, C_C:C_C + 32], ACT.Sigmoid).then_inc(sigc_ready, 1)
            act.wait_ge(x_landed, 16)
            for tok in range(TOK):
                link(act.activation(xfull[:, tok, :], xfull[:, tok, :], ACT.Square,
                                    accum_out=st[:, ST_SS + tok:ST_SS + tok + 1]))
            act.wait_ge(eps_ready, 1)
            act.activation(st[:, ST_RT:ST_RT + 2], st[:, ST_SS:ST_SS + 2], ACT.Sqrt,
                           bias=st[:, ST_EPS:ST_EPS + 1], scale=1.0 / D).then_inc(xroot_ready, 1)
            act.wait_ge(lam_ready, 1)
            act.activation(tl[:, 1, :], tl[:, 0, :], ACT.Exp, scale=-1.0).then_inc(elam_ready, 1)

            def split_hi(gr, slot_chunk, n_chunk, which, slot_gr, wait_used):
                if which == 0:
                    act.wait_ge(w_landed[slot_chunk], n_chunk)
                if wait_used:
                    act.wait_ge(gran_used, gr - (NG - 1))
                act.copy(w_hi[:, slot_gr, :, :], w_st[:, slot_chunk, which, :, :]).then_inc(hi_ready, 1)

            def split_h(s, g):
                if s > 0:
                    act.wait_ge(gran_used, s * GSB - GPT + g + 1)
                act.wait_ge(h32_ready, 4 * s + g + 1)
                act.copy(h_hi[:, 2 * g:2 * g + 2, :], h32[:, 2 * g:2 * g + 2, :]).then_inc(hh_ready, 1)

            def step(s, i, first):
                for u in range(TPI):
                    for g in range(GPT):
                        n = u * GPT + g
                        if first and n < 3:
                            for k in ((0, 1), (2,), (3,))[n]:
                                split_h(s, k)
                        c0 = s * NT * 2 + n // 2
                        gr = i * (TPI * GPT) + (s * GSB + n)
                        used = not (isinstance(gr, int) and gr < NG)
                        split_hi(gr, c0 % NW, (i * (2 * TPI // NW) + c0 // NW + 1) * 16, n % 2, n % NG, used)

            for s in range(NSB - 1):
                step(s, 0, True)
                with act.Fori(1, NI) as i:
                    step(s, i, False)

            def copy_qkT(h):
                act.wait_ge(qkT_ps, h + 1)
                if h >= 1:
                    act.wait_ge(s_ps, h)
                act.copy(qkT[:].rearrange("p a n -> p (a n)"), side[2][:]).then_inc(qkT_ready, 1)

            def exps(h):
                act.wait_ge(s_ready, 2 * h + 2)
                for tok in range(TOK):
                    act.activation(prob[:, h % 2, tok, :], prob[:, h % 2, tok, :], ACT.Exp,
                                   bias=mx[:, h % 2, tok:tok + 1], accum_out=es[:, h % 4, tok:tok + 1]).then_inc(p_ready, 1)

            def copy_probT(h):
                act.wait_ge(pT_ps, h + 1)
                act.wait_ge(o_ps, h) if h >= 1 else None
                act.copy(probT[:].rearrange("p a n -> p (a n)"), side[0][:]).then_inc(pT_ready, 1)

            def scale_o(h):
                act.wait_ge(o_ps, h + 1)
                act.wait_ge(rinv_ready, h + 1)
                for tok in range(TOK):
                    ins = act.activation(head(QB, h, tok), side[1][:, tok * P:(tok + 1) * P], ACT.Copy,
                                         scale=es[:, h % 4, tok:tok + 1])
                ins.then_inc(o_ready, 1)

            def gate_sig(t):
                if t >= 1:
                    act.wait_ge(z_ready, t)
                act.activation(sig[:], proj[:, GB + t, :, :], ACT.Sigmoid).then_inc(sig_ready, 1)

            def norm_B():
                act.wait_ge(o_ready, NH)
                for tok in range(TOK):
                    link(act.activation(proj[:, VB:VB + 4, tok, :], proj[:, QB:QB + 4, tok, :], ACT.Square,
                                        accum_out=st[:, ST_B + tok:ST_B + tok + 1]))
                act.activation(st[:, ST_BR:ST_BR + 2], st[:, ST_B:ST_B + 2], ACT.Sqrt,
                               bias=st[:, ST_EPS:ST_EPS + 1], scale=1.0 / W).then_inc(rB_ready, 1)

            def yB_upper(r):
                act.wait_ge(yBT_ps, r + 1)
                for k in range(2):
                    n = 2 * r + k
                    ins = act.activation(yB_hi[:, n, :], side[2 + r % 2][:, k * S:(k + 1) * S], ACT.Copy,
                                         scale=par[:, C_GNA + n:C_GNA + n + 1])
                ins.then_inc(yB_hi_r, 1)

            s = NSB - 1
            for g in range(GSB):
                if g < 3:
                    for k in ((0, 1), (2,), (3,))[g]:
                        split_h(s, k)
                for h in range(NH):
                    if g == copy_qkT_at(h):
                        copy_qkT(h)
                    if g == exps_at(h):
                        exps(h)
                    if g == copy_probT_at(h):
                        copy_probT(h)
                    if g == scale_o_at(h):
                        scale_o(h)
                if g == NORM_B_AT:
                    norm_B()
                if g in range(GATE_AT, GATE_AT + 8, 2):
                    gate_sig((g - GATE_AT) // 2)
                for r in range(NH // 2):
                    if g == yBT_AT + r + NG:
                        yB_upper(r)
                c0 = s * NT * 2 + g // 2
                split_hi(s * GSB + g, c0 % NW, (c0 // NW + 1) * 16, g % 2, g % NG, True)

            def lru_transposed(g):
                act.wait_ge(xaT_ps, g + 1)
                if g == 0:
                    act.wait_ge(pad_set, 2)
                else:
                    act.wait_ge(xc_ready, g)
                act.copy(xaT[:, :, 2:2 + S], side[0][:].rearrange("p (k n) -> p k n", k=2)).then_inc(xaT_ready, 1)

            def lru_gate_sigmoid(g):
                act.wait_ge(gaT_ps, g + 1)
                if g > 0:
                    act.wait_ge(y_ready, g)
                act.activation(gaS[:], side[2][:].rearrange("p (k n) -> p k n", k=2), ACT.Sigmoid).then_inc(gsig_ready, 1)

            def lru_sigmoids(g, e):
                act.wait_ge(gate_ps, 2 * g + e + 1)
                if g >= 1:
                    act.wait_ge(y_ready, g)
                    act.wait_ge(hsq_ready, g)
                for k in range(2):
                    n = e * NB + 2 * g + k
                    act.activation(rv[:, e, k, :], side[1][:, k * S:(k + 1) * S], ACT.Sigmoid,
                                   bias=par[:, C_BA + n:C_BA + n + 1]).then_inc(r_ready, 1)
                    ins = act.activation(ib[:, e, k, :], side[3][:, k * S:(k + 1) * S], ACT.Sigmoid,
                                         bias=par[:, C_BX + n:C_BX + n + 1])
                ins.then_inc(ri_ready, 1)

            def lru_decay(g):
                act.wait_ge(r_ready, 4 * g + 4)
                act.wait_ge(coef_ready, 2)
                for e in range(2):
                    for k in range(2):
                        n = e * NB + 2 * g + k
                        act.activation(wa_[:, e, k, :], rv[:, e, k, :], ACT.Exp, scale=coef[:, 1, n:n + 1])
                        ins = act.activation(rv[:, e, k, :], rv[:, e, k, :], ACT.Tanh, scale=coef[:, 0, n:n + 1])
                ins.then_inc(v_ready, 1)

            def lru_root(g):
                act.wait_ge(m_ready, g + 1)
                act.activation(rv[:], rv[:], ACT.Sqrt).then_inc(sq_ready, 1)

            def yA_upper(g):
                act.wait_ge(y_ready, g + 1)
                if g % 2 == 0:
                    act.wait_ge(gaT_ps, g + 2)
                act.copy(yA_hi[:, 2 * g:2 * g + 2, :], yA[:, 2 * g:2 * g + 2, :]).then_inc(yA_hi_r, 1)

            def norm_A():
                act.wait_ge(ssA_ps, 1)
                act.activation(st[:, ST_AR:ST_AR + 2], side[0][:, 0:2], ACT.Sqrt,
                               bias=st[:, ST_EPS:ST_EPS + 1], scale=1.0 / W).then_inc(rA_ready, 1)

            def gate_copy(n):
                act.wait_ge(gate_bc_ps, n + 1)
                m = mod if n < 4 else mod2
                act.copy(m[:, (n % 4) // 2, (n % 2) * CT:(n % 2 + 1) * CT], side[1 + n % 3][:]).then_inc(gate_ready, 1)

            def squares(t):
                act.wait_ge(t3_ready, t + 1)
                for tok in range(TOK):
                    if t + tok > 0:
                        act.wait_ge(fss_ready, 2 * t + tok)
                    act.activation(side[0][:], out_tile(t)[:, tok, :], ACT.Square,
                                   accum_out=fss[:, tok, t:t + 1]).then_inc(fss_ready, 1)

            for g in range(GOUT):
                for n in range(NB // 2):
                    k = g - LRU_STEP * n
                    if k == 4:
                        lru_transposed(n)
                    if k == LRU_GA + 4:
                        lru_gate_sigmoid(n)
                    if k in (LRU_G0 + 4, LRU_G1 + 4):
                        lru_sigmoids(n, int(k > LRU_G0 + 4))
                    if k == LRU_G1 + 4:
                        lru_decay(n)
                    if k == LRU_G1 + 6:
                        lru_root(n)
                    if k == LRU_Y + 3:
                        yA_upper(n)
                if g == NORM_A_AT + 3:
                    norm_A()
                for n in range(NCO):
                    if g == gate_bc_at(n) + 3:
                        gate_copy(n)
                    if g == evac_at(NCO + n) + 3:
                        squares(n)
                wc = NSB * NT * 2 + g // 2
                split_hi(NSB * GSB + g, wc % NW, (wc // NW + 1) * 16, g % 2, g % NG, True)
            squares(NCO - 1)
            act.wait_ge(fsum_ready, 1)
            act.activation(st[:, ST_FR:ST_FR + 2], st[:, ST_F:ST_F + 2], ACT.Sqrt,
                           bias=st[:, ST_EPS:ST_EPS + 1], scale=1.0 / D).then_inc(rF_ready, 1)

        @block.vector
        def _(dve):
            steps = [0]

            def link(ins):
                steps[0] += 1
                ins.then_inc(dve_step, 1)
                dve.wait_ge(dve_step, steps[0])

            dve.wait_ge(sigc_ready, 1)
            dve.tensor_tensor(cond[:], cond[:], par[:, C_C:C_C + 32], ALU.mult).then_inc(cond_ready, 1)
            dve.wait_ge(cond_ready, 1)
            lam = par[:, C_LAM:C_LAM + 32]
            dve.scalar_tensor_tensor(out=tl[:, 0, :], in0=lam, scalar=-1.0, in1=lam, op0=ALU.mult, op1=ALU.max).then_inc(lam_ready, 1)

            def ada(n, slot, n_land, acc_t, which, cnd, first, back):
                dve.wait_ge(a_landed[slot], n_land)
                if first:
                    dve.tensor_scalar(acc_t[:, which, :], a_st[:, slot, :], cnd, None, ALU.mult).then_inc(ada_step, 1)
                    return
                dve.wait_ge(ada_step, n - (back - 1))
                dve.scalar_tensor_tensor(out=acc_t[:, which, :], in0=a_st[:, slot, :], scalar=cnd,
                                         in1=acc_t[:, which, :], op0=ALU.mult, op1=ALU.add).then_inc(ada_step, 1)

            def ada_in(s, i, q):
                n = i * API + (s * APS + q)
                j = i * (API // 2) + q // 2
                first = isinstance(i, int) and i == 0 and q < 2
                if first and s > 0:
                    dve.wait_ge(mod_ps, s)
                cnd = cond[:, j:j + 1] if isinstance(j, int) else cond[:, bass.ds(j, 1)]
                ada(n, q % NA, (i * (API // NA) + ((s * APS + q) // NA + 1)) * 16, mod, 1 - q % 2, cnd, first, 2)

            def split_lo(gr, slot_chunk, which, slot_gr):
                dve.wait_ge(hi_ready, gr + 1)
                dve.tensor_tensor(w_lo[:, slot_gr, :, :], w_st[:, slot_chunk, which, :, :],
                                  w_hi[:, slot_gr, :, :].bitcast(F32), ALU.subtract).then_inc(lo_ready, 1)

            def split_h(s, g):
                dve.wait_ge(hh_ready, 4 * s + g + 1)
                dve.tensor_tensor(h_lo[:, 2 * g:2 * g + 2, :], h32[:, 2 * g:2 * g + 2, :],
                                  h_hi[:, 2 * g:2 * g + 2, :].bitcast(F32), ALU.subtract).then_inc(hl_ready, 1)

            def evac(s, t, tile, buf):
                n = t + s * NT
                dve.wait_ge(gran_used, n * GPT + GPT)
                if s > 0:
                    dve.wait_ge(evac_done, n - (NT - 1) if s < NSB - 1 else NT * (NSB - 1))
                for tok in range(TOK):
                    if s == 0:
                        ins = dve.tensor_copy(proj_at(tile, tok), acc[buf][tok][:])
                    else:
                        ins = dve.tensor_tensor(proj_at(tile, tok), proj_at(tile, tok), acc[buf][tok][:], ALU.add)
                ins.then_inc(evac_done, 1)

            def mod_columns(s):
                dve.wait_ge(mod_ps, s + 1)
                b0 = s * KT
                link(dve.tensor_tensor(mcols[:, 2, :], side[0][:, 0:KT], par[:, C_BSC + b0:C_BSC + b0 + KT], ALU.add))
                dve.tensor_tensor(mcols[:, 1, :], side[0][:, KT:2 * KT], par[:, C_BSH + b0:C_BSH + b0 + KT], ALU.add).then_inc(mod_cols, 1)
                dve.scalar_tensor_tensor(out=mcols[:, 0, :], in0=mcols[:, 2, :], scalar=1.0,
                                         in1=par[:, C_NG + b0:C_NG + b0 + KT], op0=ALU.add, op1=ALU.mult).then_inc(mod_cols, 1)
                dve.wait_ge(mod_cols, 2 * s + 2)

            def modulate(s, r):
                dve.wait_ge(xT_ps, 4 * s + r + 1)
                if r == 0 and s > 0:
                    dve.wait_ge(hl_ready, 4 * s)
                for k in range(2):
                    n = 2 * r + k
                    ins = dve.tensor_scalar(h32[:, n, :], side[(r + 1) % 2][:, k * S:(k + 1) * S],
                                            mcols[:, 0, n:n + 1], mcols[:, 1, n:n + 1], ALU.mult, ALU.add)
                ins.then_inc(h32_ready, 1)

            for q in range(API):
                ada_in(0, 0, q)
            dve.wait_ge(xroot_ready, 1)
            dve.reciprocal(st[:, ST_R:ST_R + 2], st[:, ST_RT:ST_RT + 2]).then_inc(rstd_ready, 1)
            with dve.Fori(1, NI) as i:
                for q in range(API):
                    ada_in(0, i, q)
            y, sr, s2, pl = (tl[:, k, :] for k in (1, 2, 3, 4))
            dve.wait_ge(elam_ready, 1)
            link(dve.tensor_scalar(sr, y, 2.0, None, ALU.add))
            link(dve.reciprocal(sr, sr))
            link(dve.tensor_tensor(sr, sr, y, ALU.mult))
            link(dve.tensor_tensor(s2, sr, sr, ALU.mult))
            link(dve.tensor_scalar(pl, s2, 1.0 / 19, None, ALU.mult))
            for k in (17, 15, 13, 11, 9, 7, 5, 3):
                link(dve.scalar_tensor_tensor(out=pl, in0=pl, scalar=1.0 / k, in1=s2, op0=ALU.add, op1=ALU.mult))
            link(dve.scalar_tensor_tensor(out=pl, in0=pl, scalar=1.0, in1=sr, op0=ALU.add, op1=ALU.mult))
            link(dve.tensor_scalar(s2, lam, -1.0, 0.0, ALU.mult, ALU.max))
            link(dve.scalar_tensor_tensor(out=pl, in0=pl, scalar=2.0, in1=s2, op0=ALU.mult, op1=ALU.add))
            dve.tensor_scalar(coef[:, 0, :], pl, C_RG / 2, None, ALU.mult).then_inc(coef_ready, 1)
            dve.tensor_scalar(coef[:, 1, :], pl, -C_RG, None, ALU.mult).then_inc(coef_ready, 1)
            mod_columns(0)
            for r in range(4):
                modulate(0, r)

            def step(s, i, first, last):
                for u in range(TPI):
                    for g in range(GPT):
                        n = u * GPT + g
                        if first and n == 1 and s > 0:
                            modulate(s, 3)
                        if first and n < 3:
                            for k in ((0, 1), (2,), (3,))[n]:
                                split_h(s, k)
                        if g % 2 == 0:
                            for q in ada_with(n // 2, last):
                                ada_in(s + 1, i, q)
                        if last and n == 7:
                            mod_columns(s + 1)
                            modulate(s + 1, 0)
                        if last and n in (10, 11):
                            modulate(s + 1, n - 9)
                        c0 = s * NT * 2 + n // 2
                        split_lo(i * (TPI * GPT) + (s * GSB + n), c0 % NW, n % 2, n % NG)
                    if first and u == 0:
                        if s == 0:
                            dve.wait_ge(rstd_ready, 1)
                            dve.wait_ge(mask_stored, 16)
                        else:
                            evac(s - 1, NT - 1, NT - 1, (NT - 1) % 3)
                    else:
                        evac(s, i * TPI + (u - 1), i * TPI + (u - 1), (u - 1) % 3)

            for s in range(NSB - 1):
                step(s, 0, True, False)
                with dve.Fori(1, NI - 1) as i:
                    step(s, i, False, False)
                step(s, NI - 1, False, True)

            def add_bias(h):
                dve.wait_ge(s_ps, h + 1)
                dve.wait_ge(bias_landed[h % 2], 16 * ROWS * (h // 2 + 1))
                if h >= 2:
                    dve.wait_ge(pT_ps, h - 1)
                dve.scalar_tensor_tensor(out=prob[:, h % 2, :, :], in0=side[3][:].rearrange("p (t n) -> p t n", t=TOK),
                                         scalar=SCALE, in1=bias[:, h % 2, :, :], op0=ALU.mult, op1=ALU.add).then_inc(s_ready, 1)
                dve.wait_ge(s_ready, 2 * h + 1)
                link(dve.tensor_reduce(mx[:, h % 2, :], prob[:, h % 2, :, :], AX, ALU.max))
                dve.tensor_scalar(mx[:, h % 2, :], mx[:, h % 2, :], -1.0, None, ALU.mult).then_inc(s_ready, 1)

            def rinv(h):
                dve.wait_ge(p_ready, 2 * h + 2)
                dve.reciprocal(es[:, h % 4, :], es[:, h % 4, :]).then_inc(rinv_ready, 1)

            def gate_z(t):
                dve.wait_ge(sig_ready, t + 1)
                link(dve.tensor_tensor(sig[:], sig[:], proj[:, GB + t, :, :], ALU.mult))
                dve.tensor_tensor(proj[:, GB + t, :, :], sig[:], proj[:, QB + t, :, :], ALU.mult).then_inc(z_ready, 1)

            def yB_lower(r):
                dve.wait_ge(yB_hi_r, r + 1)
                for k in range(2):
                    n = 2 * r + k
                    ins = dve.scalar_tensor_tensor(out=yB_lo[:, n, :], in0=side[2 + r % 2][:, k * S:(k + 1) * S],
                                                   scalar=par[:, C_GNA + n:C_GNA + n + 1],
                                                   in1=yB_hi[:, n, :].bitcast(F32), op0=ALU.mult, op1=ALU.subtract)
                ins.then_inc(yB_lo_r, 1)

            s = NSB - 1
            for g in range(GSB):
                t = g // GPT
                if g == 1:
                    modulate(s, 3)
                if g < 3:
                    for k in ((0, 1), (2,), (3,))[g]:
                        split_h(s, k)
                for q in half_of(gate1_with(g // 2), g % 2):
                    if q < 2:
                        dve.wait_ge(gbias_landed, 16)
                    ada(NSB * APS + q, q % NA, ((NSB * APS + q) // NA + 1) * 16, mod, q % 2, cond[:, q // 2:q // 2 + 1], False, 2)
                for h in range(NH):
                    if g == add_bias_at(h):
                        add_bias(h)
                    if g == rinv_at(h):
                        rinv(h)
                if g in range(GATE_AT, GATE_AT + 8, 2):
                    gate_z((g - GATE_AT) // 2)
                for r in range(NH // 2):
                    if g == yBT_AT + r + NG:
                        yB_lower(r)
                c0 = s * NT * 2 + g // 2
                split_lo(s * GSB + g, c0 % NW, g % 2, g % NG)
                if g % GPT == GPT - 1:
                    if t == 0:
                        evac(s - 1, NT - 1, NT - 1, (NT - 1) % 3)
                    else:
                        evac(s, t - 1, LAST[t - 1], (t - 1) % 2)

            def convolve(g, k):
                dve.wait_ge(xaT_ready, g + 1)
                if g >= 2:
                    dve.wait_ge(ixc_ready, 2 * g - 2)
                b = 2 * g + k
                for j in range(CONV_W):
                    n = C_CW + j * NB + b
                    src = xaT[:, k, j:j + S]
                    if j == 0:
                        ins = dve.tensor_scalar(xc[:, g % 2, k, :], src, par[:, n:n + 1], par[:, C_CB + b:C_CB + b + 1],
                                                ALU.mult, ALU.add)
                    else:
                        ins = dve.scalar_tensor_tensor(out=xc[:, g % 2, k, :], in0=src, scalar=par[:, n:n + 1],
                                                       in1=xc[:, g % 2, k, :], op0=ALU.mult, op1=ALU.add)
                    if j < CONV_W - 1:
                        link(ins)
                if k == 1:
                    ins.then_inc(xc_ready, 1)

            def gate_silu(g):
                dve.wait_ge(gsig_ready, g + 1)
                dve.tensor_tensor(gaS[:], gaS[:], side[2][:].rearrange("p (k n) -> p k n", k=2), ALU.mult).then_inc(gaS_ready, 1)

            def flat(t):
                return t[:].rearrange("p e k n -> p (e k n)")

            def decay(g):
                dve.wait_ge(v_ready, g + 1)
                dve.wait_ge(ixc_ready, 2 * g + 2)
                dve.scalar_tensor_tensor(out=flat(ib), in0=flat(wa_), scalar=1.0, in1=flat(ib), op0=ALU.add,
                                         op1=ALU.mult).then_inc(b_ready, 1)
                dve.scalar_tensor_tensor(out=flat(wa_), in0=flat(wa_), scalar=1.0, in1=flat(rv), op0=ALU.add,
                                         op1=ALU.mult).then_inc(m_ready, 1)

            def inputs(g):
                dve.wait_ge(m_ready, g + 1)
                dve.tensor_scalar(wa_[:], wa_[:], -1.0, 1.0, ALU.mult, ALU.add).then_inc(a_ready, 1)
                dve.wait_ge(sq_ready, g + 1)
                dve.wait_ge(b_ready, 2 * g + 1)
                dve.tensor_tensor(ib[:], ib[:], rv[:], ALU.mult).then_inc(b_ready, 1)

            def scans(g):
                dve.wait_ge(b_ready, 2 * g + 2)
                dve.wait_ge(a_ready, g + 1)
                for k in range(2):
                    dve.tensor_tensor_scan(rv[:, 0, k, :], wa_[:, 0, k, :], ib[:, 0, k, :], 0.0, ALU.mult, ALU.add).then_inc(scan_ready, 1)
                    dve.tensor_tensor_scan(rv[:, 1, k, ::-1], wa_[:, 1, k, ::-1], ib[:, 1, k, ::-1], 0.0,
                                           ALU.mult, ALU.add).then_inc(scan_ready, 1)
                dve.wait_ge(scan_ready, 4 * g + 4)
                dve.tensor_tensor(rv[:, 0, :, :], rv[:, 0, :, :], rv[:, 1, :, :], ALU.add).then_inc(h_ready, 1)

            def gated(g):
                dve.wait_ge(h_ready, g + 1)
                dve.wait_ge(gaS_ready, g + 1)
                if g % 2 == 0:
                    dve.wait_ge(xaT_ps, g + 2)
                for k in range(2):
                    b = 2 * g + k
                    ins = dve.scalar_tensor_tensor(out=yA[:, b, :], in0=rv[:, 0, k, :],
                                                   scalar=par[:, C_GNL + b:C_GNL + b + 1], in1=gaS[:, k, :],
                                                   op0=ALU.mult, op1=ALU.mult)
                ins.then_inc(y_ready, 1)

            def yA_lower(g):
                dve.wait_ge(yA_hi_r, g + 1)
                dve.tensor_tensor(yA_lo[:, 2 * g:2 * g + 2, :], yA[:, 2 * g:2 * g + 2, :],
                                  yA_hi[:, 2 * g:2 * g + 2, :].bitcast(F32), ALU.subtract).then_inc(yA_lo_r, 1)

            def evac_out(o):
                n = NSB * GSB + (o + 1) * GPO
                dve.wait_ge(gran_used, n)
                t = out_tile(o % NCO)
                if o == 0:
                    dve.wait_ge(rB_ready, 1)
                    link(dve.reciprocal(st[:, ST_BR:ST_BR + 2], st[:, ST_BR:ST_BR + 2]))
                if o == NCO:
                    dve.wait_ge(rA_ready, 1)
                    link(dve.reciprocal(st[:, ST_AR:ST_AR + 2], st[:, ST_AR:ST_AR + 2]))
                if o >= NCO:
                    dve.wait_ge(evac_done, NSB * NT + o - NCO + 1)
                for tok in range(TOK):
                    if o < NCO:
                        ins = dve.tensor_scalar(t[:, tok, :], acc[o % 2][tok][:], st[:, ST_BR + tok:ST_BR + tok + 1], None, ALU.mult)
                    else:
                        ins = dve.scalar_tensor_tensor(out=t[:, tok, :], in0=acc[o % 2][tok][:],
                                                       scalar=st[:, ST_AR + tok:ST_AR + tok + 1], in1=t[:, tok, :],
                                                       op0=ALU.mult, op1=ALU.add)
                ins.then_inc(evac_done, 1)

            for g in range(GOUT):
                for n in range(NB // 2):
                    k = g - LRU_STEP * n
                    if k in (4, 5):
                        convolve(n, k - 4)
                    if k == LRU_GA + 4:
                        gate_silu(n)
                    if k == LRU_G1 + 5:
                        decay(n)
                    if k == LRU_G1 + 6:
                        inputs(n)
                    if k == LRU_Y:
                        scans(n)
                        gated(n)
                    if k == LRU_Y + 3:
                        yA_lower(n)
                split_lo(NSB * GSB + g, (NSB * NT * 2 + g // 2) % NW, g % 2, g % NG)
                for q in half_of(gate2_with(g // 2), g % 2):
                    if q == 0:
                        dve.wait_ge(gbias_landed, 32)
                    cn, j = (NSB + 1) * APS + q, q % (APS // 2)
                    ada(cn, cn % NA, (cn // NA + 1) * 16, mod2, q // (APS // 2), cond[:, j:j + 1], False, 1)
                if g == GPT - 1:
                    evac(NSB - 1, NT - 1, LAST[NT - 1], (NT - 1) % 2)
                for o in range(2 * NCO - 1):
                    if g == evac_at(o):
                        evac_out(o)
            evac_out(2 * NCO - 1)
            dve.wait_ge(fss_ready, 2 * NCO)
            dve.tensor_reduce(st[:, ST_F:ST_F + 2], fss[:], AX, ALU.add).then_inc(fsum_ready, 1)
            dve.wait_ge(rF_ready, 1)
            link(dve.reciprocal(st[:, ST_FR:ST_FR + 2], st[:, ST_FR:ST_FR + 2]))
            for t in range(NCO):
                dve.wait_ge(t4_ready, t + 1)
                for tok in range(TOK):
                    ins = dve.tensor_scalar(out_tile(t)[:, tok, :], out_tile(t)[:, tok, :],
                                            st[:, ST_FR + tok:ST_FR + tok + 1], None, ALU.mult)
                ins.then_inc(fin_ready, 1)

        @block.tensor
        def _(pe):
            pe.wait_ge(consts_ready, 2)
            pe.wait_ge(par_landed, 16 * 10)
            pe.transpose(side[0][:, 0:P], par_rows[:, 0, :], ident[:])
            pe.transpose(side[0][:, P:2 * P], par_rows[:, 1, :], ident[:])
            pe.transpose(side[0][:, 2 * P:NPAR], par_rows[0:NPAR - 2 * P, 2, :],
                         ident[0:NPAR - 2 * P, 0:NPAR - 2 * P]).then_inc(par_ps, 1)

            def granule(slot, up, low, k0, buf, first, last, gr):
                pe.wait_ge(lo_ready, gr + 1)
                for k in range(GK):
                    for tok in range(TOK):
                        lh = up[:, k0 + k, tok * P:(tok + 1) * P]
                        ll = low[:, k0 + k, tok * P:(tok + 1) * P]
                        pe.matmul(acc[buf][tok][:], lh, w_hi[:, slot, k, :], start=first and k == 0, stop=False)
                        pe.matmul(acc[buf][tok][:], lh, w_lo[:, slot, k, :], start=False, stop=False)
                        ins = pe.matmul(acc[buf][tok][:], ll, w_hi[:, slot, k, :], start=False, stop=last and k == GK - 1)
                ins.then_inc(gran_used, 1)

            def mod_sums(s):
                pe.wait_ge(ada_step, APS * (s + 1))
                if s == 0:
                    pe.wait_ge(par_ready, 1)
                else:
                    pe.wait_ge(h32_ready, 4 * s)
                for k in range(2 * KT):
                    ins = pe.matmul(side[0][:, k:k + 1], mod[:, k // KT, (k % KT) * P:(k % KT + 1) * P], ones[:, 0:1],
                                    start=True, stop=True)
                ins.then_inc(mod_ps, 1)

            def transpose_x(s, r):
                pe.wait_ge(xs_scaled, 2 * (s + 1))
                if r == 1:
                    pe.wait_ge(mod_cols, 2 * s + 2)
                if r >= 2:
                    pe.wait_ge(h32_ready, 4 * s + r - 1)
                for k in range(2):
                    for tok in range(TOK):
                        ins = pe.transpose(side[(r + 1) % 2][:, k * S + tok * P:k * S + (tok + 1) * P],
                                           xs[:, tok, (2 * r + k) * P:(2 * r + k + 1) * P], ident[:])
                ins.then_inc(xT_ps, 1)

            mod_sums(0)
            for r in range(4):
                transpose_x(0, r)

            def step(s, i, first, last):
                for u in range(TPI):
                    n = i * TPI + (s * NT + u)
                    if not (isinstance(n, int) and n < 3):
                        pe.wait_ge(evac_done, n - 2)
                    for g in range(GPT):
                        if first and u == 0:
                            pe.wait_ge(hl_ready, 4 * s + g + 1)
                        n = u * GPT + g
                        if last and n == 4:
                            mod_sums(s + 1)
                            transpose_x(s + 1, 0)
                        if last and n in (7, 8, 10):
                            transpose_x(s + 1, (7, 8, 10).index(n) + 1)
                        gr = i * (TPI * GPT) + (s * GSB + n)
                        granule((u * GPT + g) % NG, h_hi, h_lo, GK * g, u, g == 0, g == GPT - 1, gr)

            for s in range(NSB - 1):
                step(s, 0, True, False)
                with pe.Fori(1, NI - 1) as i:
                    step(s, i, False, False)
                step(s, NI - 1, False, True)

            def transpose_qk(h):
                if h == 0:
                    pe.wait_ge(hl_ready, 4 * NSB)
                tile = 3 * (h // 4) + 2
                pe.wait_ge(evac_done, (NSB - 1) * NT + tile + 1)
                if h >= 1:
                    pe.wait_ge(qkT_ready, h)
                for a, part in enumerate((QB, KB)):
                    for tok in range(TOK):
                        ins = pe.transpose(side[2][:, a * S + tok * P:a * S + (tok + 1) * P], head(part, h, tok), ident[:])
                ins.then_inc(qkT_ps, 1)

            def scores(h):
                pe.wait_ge(qkT_ready, h + 1)
                if h >= 1:
                    pe.wait_ge(s_ready, 2 * h - 1)
                for tok in range(TOK):
                    ins = pe.matmul(side[3][:, tok * S:(tok + 1) * S], qkT[:, 0, tok * P:(tok + 1) * P], qkT[:, 1, :],
                                    start=True, stop=True)
                ins.then_inc(s_ps, 1)

            def transpose_p(h):
                pe.wait_ge(p_ready, 2 * h + 2)
                if h >= 1:
                    pe.wait_ge(pT_ready, h)
                for kt in range(2):
                    for tok in range(TOK):
                        ins = pe.transpose(side[0][:, kt * S + tok * P:kt * S + (tok + 1) * P],
                                           prob[:, h % 2, tok, kt * P:(kt + 1) * P], ident[:])
                ins.then_inc(pT_ps, 1)

            def p_times_v(h):
                pe.wait_ge(pT_ready, h + 1)
                if h >= 1:
                    pe.wait_ge(o_ready, h)
                for tok in range(TOK):
                    for kt in range(2):
                        ins = pe.matmul(side[1][:, tok * P:(tok + 1) * P], probT[:, kt, tok * P:(tok + 1) * P],
                                        head(VB, h, kt), start=(kt == 0), stop=(kt == 1))
                ins.then_inc(o_ps, 1)

            def transpose_yB(r):
                pe.wait_ge(z_ready, r // 2 + 1)
                if r == 0:
                    pe.wait_ge(s_ready, 2 * NH)
                if r >= 2:
                    pe.wait_ge(yB_lo_r, r - 1)
                for k in range(2):
                    for tok in range(TOK):
                        ins = pe.transpose(side[2 + r % 2][:, k * S + tok * P:k * S + (tok + 1) * P],
                                           head(GB, 2 * r + k, tok), ident[:])
                ins.then_inc(yBT_ps, 1)

            s = NSB - 1
            for g in range(GSB):
                t = g // GPT
                for h in range(NH):
                    if g == qk_at(h):
                        transpose_qk(h)
                    if g == scores_at(h):
                        scores(h)
                    if g == pT_at(h):
                        transpose_p(h)
                    if g == pv_at(h):
                        p_times_v(h)
                for r in range(NH // 2):
                    if g == yBT_AT + r:
                        transpose_yB(r)
                if g % GPT == 0:
                    pe.wait_ge(evac_done, s * NT + t - 1)
                if g < GPT:
                    pe.wait_ge(hl_ready, 4 * s + g + 1)
                granule(g % NG, h_hi, h_lo, GK * (g % GPT), t % 2, g % GPT == 0, g % GPT == GPT - 1, s * GSB + g)

            def transpose_lru(g, part, bank, done):
                if g == 0:
                    pe.wait_ge(evac_done, (NSB - 1) * NT + NT - 1 if part == XB else NSB * NT)
                    pe.wait_ge(yB_lo_r, NH // 2)
                    pe.wait_ge(o_ready, NH)
                elif part == XB:
                    pe.wait_ge(xaT_ready, g)
                else:
                    pe.wait_ge(gaS_ready, g)
                for k in range(2):
                    for tok in range(TOK):
                        b = (2 * g + k) % 4
                        ins = pe.transpose(side[bank][:, k * S + tok * P:k * S + (tok + 1) * P],
                                           proj[:, part + g // 2, tok, b * P:(b + 1) * P], ident[:])
                ins.then_inc(done, 1)

            def lru_gates(g, e):
                pe.wait_ge(xc_ready, g + 1)
                pe.wait_ge(gwt_landed[g % 2], 64 * (g // 2 + 1))
                if g + e > 0:
                    pe.wait_ge(ri_ready, 2 * g + e)
                for k in range(2):
                    bank = side[(1, 3)[k]]
                    for n in range(2):
                        ins = pe.matmul(bank[:, n * S:(n + 1) * S], gate_wt[g % 2][:, k, e, n, :], xc[:, g % 2, n, :],
                                        start=True, stop=True)
                ins.then_inc(gate_ps, 1)

            def sum_squares_A():
                pe.wait_ge(hacc_ready, NB // 2)
                pe.wait_ge(xaT_ready, NB // 2)
                for tok in range(TOK):
                    for k in range(2):
                        ins = pe.matmul(side[0][:, tok:tok + 1], hacc[:, k, tok * P:(tok + 1) * P], ones[:, 0:1],
                                        start=(k == 0), stop=(k == 1))
                ins.then_inc(ssA_ps, 1)

            def gate_broadcast(n):
                if n == 0:
                    pe.wait_ge(ada_step, (NSB + 1) * APS)
                    pe.wait_ge(ri_ready, NB)
                    pe.wait_ge(gaS_ready, NB // 2)
                if n == 4:
                    pe.wait_ge(ada_step, (NSB + 1) * APS + APS // 2)
                if n == 6:
                    pe.wait_ge(ada_step, (NSB + 2) * APS)
                if n >= 3:
                    pe.wait_ge(gate_ready, n - 2)
                m = mod if n < 4 else mod2
                pe.matmul(side[1 + n % 3][:], ones[:], m[:, (n % 4) // 2, (n % 2) * CT:(n % 2 + 1) * CT],
                          start=True, stop=True).then_inc(gate_bc_ps, 1)

            for g in range(GOUT):
                for n in range(NB // 2):
                    k = g - LRU_STEP * n
                    if k == 0:
                        transpose_lru(n, XB, 0, xaT_ps)
                    if k == LRU_GA:
                        transpose_lru(n, GA, 2, gaT_ps)
                    if k in (LRU_G0, LRU_G1):
                        lru_gates(n, int(k > LRU_G0))
                if g == NORM_A_AT:
                    sum_squares_A()
                for n in range(NCO):
                    if g == gate_bc_at(n):
                        gate_broadcast(n)
                o, k = g // GPO, g % GPO
                if k == 0:
                    pe.wait_ge(evac_done, NSB * NT + o - 1)
                if o == 0:
                    pe.wait_ge(yB_lo_r, k + 1)
                if o == NCO:
                    pe.wait_ge(yA_lo_r, k + 1)
                up, low = (yB_hi, yB_lo) if o < NCO else (yA_hi, yA_lo)
                granule(g % NG, up, low, GK * k, o % 2, k == 0, k == GPO - 1, NSB * GSB + g)


def qk_at(h): return 3 * h + 17
def copy_qkT_at(h): return qk_at(h) + 3
def scores_at(h): return qk_at(h) + 5
def add_bias_at(h): return scores_at(h) + 3
def exps_at(h): return add_bias_at(h) + 1
def pT_at(h): return exps_at(h) + 2
def copy_probT_at(h): return pT_at(h) + 3
def pv_at(h): return copy_probT_at(h) + 1
def rinv_at(h): return pv_at(h) + 1
def scale_o_at(h): return pv_at(h) + 3


GATE_AT = scale_o_at(NH - 1) + 1
NORM_B_AT = GATE_AT + 2
yBT_AT = GATE_AT + 1
LRU_STEP = 7
LRU_G0, LRU_G1 = 5, 8
LRU_GA = 7
LRU_Y = LRU_G1 + 7
NORM_A_AT = (NB // 2 - 1) * LRU_STEP + LRU_Y + 4


def evac_at(o): return (o + 1) * GPO + 3
def gate_bc_at(n): return NCO * GPO + (10 + n if n < 4 else 41 + (n - 4) if n < 6 else 58 + (n - 6))


def ada_with(n, last):
    share = (4, 4, 0, 0, 0, 0) if last else (2, 1, 1, 2, 1, 1)
    return list(range(sum(share[:n]), sum(share[:n + 1])))


def half_of(chunks, second):
    cut = (len(chunks) + 1) // 2
    return chunks[cut:] if second else chunks[:cut]


def gate1_with(n):
    return list(range(4 * n // 3, min(4 * (n + 1) // 3, APS)))


def gate_wt_with(g):
    return 3 * g if g < 2 else (LRU_STEP * (g - 2) + LRU_G1 + 12) // 2


def gate2_with(n):
    at = [min(APS, max(0, k - 3) * APS // (GOUT // WCH - 8)) for k in (n, n + 1)]
    return list(range(*at))


_OUT = ((1, S, D), 'float32')
_NAMES = ['x', 'c', 'norm_g', 'w_ada', 'b_ada', 'w_in', 'conv_w', 'conv_b', 'lru_wa', 'lru_ba', 'lru_wx', 'lru_bx',
          'lru_lambda', 'rpb', 'gn_lru', 'gn_att', 'w_out', 'final_g']


def kernel(**inputs):
    import numpy as np
    import concourse.bacc as bacc
    from concourse.bass_utils import run_bass_kernel_spmd

    nc = bacc.Bacc("TRN2", target_bir_lowering=False, num_devices=1)
    arrays, args = {}, []
    for name in _NAMES:
        a = np.ascontiguousarray(inputs[name])
        arrays[f"in_{name}"] = a
        args.append(nc.dram_tensor(f"in_{name}", a.shape, mybir.dt.from_np(a.dtype), kind="ExternalInput").ap())
    out = nc.dram_tensor("out_0", _OUT[0], F32, kind="ExternalOutput").ap()
    build(nc, *args, out)
    r = run_bass_kernel_spmd(nc, [arrays], core_ids=[0])
    return r.results[0]["out_0"]
```

```python
from concourse import mybir
import concourse.bass as bass

ALU = mybir.AluOpType
ACT = mybir.ActivationFunctionType
AX = mybir.AxisListType.X
F32 = mybir.dt.float32
F32R = mybir.dt.float32r

P = 128
D = 4096
S = 256
TOK = S // P
W = 2048
D_IN = 6 * W
NB = 16
CONV_W = 4
C_RG = 8.0
NH = 16
GW = 64
ROWS = S // GW
WIN_R, WIN_C = 8, 16
NRO = 2 * ROWS - 1
RO0 = WIN_R - ROWS
EPS = 1e-6
MASK = -1e30
SCALE = float(P) ** -0.5

NSB = 4
KT = D // P // NSB
SBW = KT * P
CT = 512
NT = D_IN // CT
GK = 2
GPT = KT // GK
WCH = 2
NW = 3
NG = 3
NA = 4
TPI = 3
NI = NT // TPI
API = 8
APS = NI * API
GSB = NT * GPT
NCO = D // CT
GPO = W // P // GK
GOUT = 2 * NCO * GPO
QB, KB, VB, GB, XB, GA = 8, 12, 16, 20, 0, 4
LAST = [QB, KB, VB, QB + 1, KB + 1, VB + 1, QB + 2, KB + 2, VB + 2, QB + 3, KB + 3, VB + 3,
        GB, GB + 1, GB + 2, GB + 3, 0, 1, 2, 3, GA, GA + 1, GA + 2, GA + 3]

C_C, C_NG, C_BSH, C_BSC = 0, 32, 64, 96
C_CW, C_CB, C_GNL, C_BA = 128, 192, 208, 224
C_BX, C_LAM, C_GNA = 256, 288, 320
NPAR = 336


def build(nc, x, c, norm_g, w_ada, b_ada, w_in, conv_w, conv_b, lru_wa, lru_ba, lru_wx, lru_bx,
          lru_lambda, rpb, gn_lru, gn_att, w_out, final_g, out):
    top = [(nc.sbuf_base + 31) // 32 * 32]

    def region(size):
        at = top[0]
        top[0] += (size + 31) // 32 * 32
        assert top[0] <= nc.sbuf_usable_end, top[0]
        return at

    def place(name, shape, at, dt=F32):
        return nc.alloc_sbuf_tensor_at(name, [P] + shape, dt, offset=at)

    def sem(name):
        return nc.alloc_semaphore(name)

    TB = TOK * CT * 4
    at_p = region(NT * TB)
    at_h = region(2 * KT * S * 4)
    at_h32 = region(KT * S * 4 + 32)
    at_xs = region(TOK * SBW * 4)
    at_mod = region(2 * SBW * 4)
    at_wst = region(NW * WCH * GK * CT * 4)
    at_ast = region(NA * SBW * 4)
    at_whi = region(NG * GK * CT * 4)
    at_wlo = region(NG * GK * CT * 4)

    proj = place("proj", [NT, TOK, CT], at_p)
    h_hi = place("h_hi", [KT, S], at_h, F32R)
    h_lo = place("h_lo", [KT, S], at_h + KT * S * 4, F32R)
    xs = place("xs", [TOK, SBW], at_xs)
    h32 = place("h32", [KT, S], at_h32)
    mod = place("mod", [2, SBW], at_mod)
    w_st = place("w_st", [NW, WCH, GK, CT], at_wst)
    a_st = place("a_st", [NA, SBW], at_ast)
    w_hi = place("w_hi", [NG, GK, CT], at_whi, F32R)
    w_lo = place("w_lo", [NG, GK, CT], at_wlo, F32R)
    xfull = place("xfull", [TOK, D], at_p)
    xsq = place("xsq", [TOK, D], at_p + TOK * D * 4)
    maskfill = place("maskfill", [GW * NH * NRO * GW // P], at_p + GB * TB)
    qkT = place("qkT", [2, S], at_xs)
    prob = place("prob", [2, TOK, S], at_xs + 2048)
    probT = place("probT", [2, S], at_xs + 6144)
    bias = place("bias", [2, TOK, S], at_h32)
    sig = place("sig", [TOK, CT], at_h32 + 4096)
    yB_hi = place("yB_hi", [NH, S], at_p + KB * TB, F32R)
    yB_lo = place("yB_lo", [NH, S], at_p + VB * TB, F32R)
    yA_hi = place("yA_hi", [NB, S], at_p + GA * TB, F32R)
    yA_lo = place("yA_lo", [NB, S], at_p + XB * TB, F32R)
    yA = place("yA", [NB, S], at_p + XB * TB)
    XPAD = S + 4
    xaT = place("xaT", [2, XPAD], at_h)
    gaS = place("gaS", [2, S], at_h + 2080)
    xc = place("xc", [2, 2, S], at_h + 4128)
    hh = place("hh", [2, S], at_h + 8224)
    hacc = place("hacc", [2, S], at_h + 10272)
    rv = place("rv", [2, 2, S], at_h + 12320)
    ib = place("ib", [2, 2, S], at_h + 16416)
    wa_ = place("wa_", [2, 2, S], at_h + 20512)
    fing = place("fing", [D], at_h)
    xres = place("xres", [2, TOK, CT], at_h32)
    mod2 = place("mod2", [2, SBW], at_xs)
    at_gw = region(4096)
    gate_wt = [place("gate_wt0", [2, 2, 2, P], at_gw), place("gate_wt1", [2, 2, 2, P], at_p + (GB + 3) * TB)]
    ident = place("ident", [P], region(512))
    ones = place("ones", [P], region(512))
    par_rows = place("par_rows", [3, P], at_gw)
    par = place("par", [NPAR], region(NPAR * 4))
    cond = place("cond", [32], region(128))
    mcols = place("mcols", [3, KT], region(96))
    coef = place("coef", [2, 32], region(256))
    tl = place("tl", [5, 32], region(640))
    st = place("st", [64], region(256))
    fss = place("fss", [TOK, NCO], region(64))
    mx = place("mx", [2, TOK], region(32))
    es = place("es", [4, TOK], region(32))
    ST_SS, ST_RT, ST_R, ST_EPS, ST_B, ST_BR, ST_A, ST_AR, ST_F, ST_FR, ST_BP = 0, 2, 4, 6, 8, 10, 12, 14, 16, 18, 32

    banks = [nc.alloc_psum_tensor(f"bank{i}", [P, 512], F32) for i in range(8)]
    acc = [banks[0:2], banks[2:4], banks[4:6]]
    side = [banks[6], banks[7], banks[4], banks[5]]

    bias_img = nc.dram_tensor("bias_img", (GW, NH, NRO, GW), F32, kind="Internal").ap()

    w_landed = [sem(f"w_landed{i}") for i in range(NW)]
    a_landed = [sem(f"a_landed{i}") for i in range(NA)]
    hi_ready, lo_ready, gran_used = sem("hi_ready"), sem("lo_ready"), sem("gran_used")
    evac_done, evac_B_done, ada_step = sem("evac_done"), sem("evac_B_done"), sem("ada_step")
    mod_ps, mod_cols, xs_landed, xs_scaled = sem("mod_ps"), sem("mod_cols"), sem("xs_landed"), sem("xs_scaled")
    xT_ps, h32_ready, hh_ready, hl_ready = sem("xT_ps"), sem("h32_ready"), sem("hh_ready"), sem("hl_ready")
    par_landed, par_ps, par_ready, cond_ready = sem("par_landed"), sem("par_ps"), sem("par_ready"), sem("cond_ready")
    consts_ready, x_landed, rstd_ready = sem("consts_ready"), sem("x_landed"), sem("rstd_ready")
    coef_ready, eps_ready = sem("coef_ready"), sem("eps_ready")
    mask_set, mask_stored, img_stored = sem("mask_set"), sem("mask_stored"), sem("img_stored")
    bias_landed = [sem("bias_landed0"), sem("bias_landed1")]
    qkT_ps, qkT_ready, s_ps, s_ready = sem("qkT_ps"), sem("qkT_ready"), sem("s_ps"), sem("s_ready")
    p_ready, pT_ps, pT_ready, o_ps, o_ready = sem("p_ready"), sem("pT_ps"), sem("pT_ready"), sem("o_ps"), sem("o_ready")
    rinv_ready = sem("rinv_ready")
    sig_ready, z_ready, yBT_ps, yB_hi_r, yB_lo_r = sem("sig_ready"), sem("z_ready"), sem("yBT_ps"), sem("yB_hi_r"), sem("yB_lo_r")
    ssB_part, ssB_ready = sem("ssB_part"), sem("ssB_ready")
    rB_ready, rB_inv, rA_ready = sem("rB_ready"), sem("rB_inv"), sem("rA_ready")
    xaT_ps, gaT_ps, xaT_ready, gsig_ready, gaS_ready = sem("xaT_ps"), sem("gaT_ps"), sem("xaT_ready"), sem("gsig_ready"), sem("gaS_ready")
    pad_set, xc_ready, gate_ps, ri_ready, v_ready = sem("pad_set"), sem("xc_ready"), sem("gate_ps"), sem("ri_ready"), sem("v_ready")
    gwt_landed = [sem("gwt_landed0"), sem("gwt_landed1")]
    r_ready, m_ready, b_ready, sq_ready, scan_ready, h_ready, y_ready = sem("r_ready"), sem("m_ready"), sem("b_ready"), sem("sq_ready"), sem("scan_ready"), sem("h_ready"), sem("y_ready")
    a_ready, yA_hi_r, yA_lo_r, hacc_ready, ssA_ps = sem("a_ready"), sem("yA_hi_r"), sem("yA_lo_r"), sem("hacc_ready"), sem("ssA_ps")
    hsq_ready = sem("hsq_ready")
    gzero, gbias_landed, gate_bc_ps, gate_ready = sem("gzero"), sem("gbias_landed"), sem("gate_bc_ps"), sem("gate_ready")
    fing_landed, ixc_ready = sem("fing_landed"), sem("ixc_ready")
    xres_landed = [sem("xres_landed0"), sem("xres_landed1")]
    last_ready, sum_ready, rF_inv = sem("last_ready"), sem("sum_ready"), sem("rF_inv")
    t3_ready, fss_ready, t4_ready, rF_ready, fin_dve, fin_act, out_stored = (
        sem("t3_ready"), sem("fss_ready"), sem("t4_ready"), sem("rF_ready"), sem("fin_dve"), sem("fin_act"), sem("out_stored"))
    sigc_ready, xroot_ready, lam_ready, elam_ready, fsum_ready = (
        sem("sigc_ready"), sem("xroot_ready"), sem("lam_ready"), sem("elam_ready"), sem("fsum_ready"))
    dve_step, act_step, pool_step = sem("dve_step"), sem("act_step"), sem("pool_step")

    x_v = x.rearrange("b (t p) d -> p (b t) d", p=P)
    out_v = out.rearrange("b (t p) d -> p (b t) d", p=P)
    w_in_v = w_in.rearrange("l (k p) n -> p (l k) n", p=P)
    w_ada_v = w_ada.rearrange("l (k p) n -> p (l k) n", p=P)
    w_out_v = w_out.rearrange("l (k p) n -> p (l k) n", p=P)
    b_gate = b_ada[:, 2 * D:3 * D]

    def xT_bank(s, r):
        return (side[1], banks[2], banks[3], banks[4])[r] if s == 0 else side[(r + 1) % 2]

    def proj_at(t, tok=None):
        if isinstance(t, int):
            v = proj[:, t, :, :]
        else:
            v = proj[:, bass.ds(t, 1), :, :].rearrange("p a t n -> p (a t) n")
        return v if tok is None else v[:, tok, :]

    def head(part, h, tok):
        return proj[:, part + h // 4, tok, (h % 4) * P:(h % 4 + 1) * P]

    def out_tile(o):
        return proj[:, (QB + o) if o < 4 else (GB + o - 4), :, :]

    def gate_cols(t):
        return (mod if t < 4 else mod2)[:, (t % 4) // 2, (t % 2) * CT:(t % 2 + 1) * CT]

    block = nc.Block()
    with block:
        @block.sync
        def _(sp):
            def w_in_chunk(s, i, tile_col, u, half):
                base = s * NT * 2 + 2 * u + half
                n = i * (2 * TPI) + base
                k0 = s * KT + half * WCH * GK
                src = w_in_v[:, k0:k0 + WCH * GK, bass.ds(tile_col * CT, CT)]
                if not (isinstance(n, int) and n < NW):
                    sp.wait_ge(lo_ready, n * 2 - 4)
                sp.dma_start(w_st[:, base % NW, :, :, :].rearrange("p a b n -> p (a b) n"), src).then_inc(w_landed[base % NW], 16)

            def ada_dma(n0, i, q, col0):
                n = i * API + (n0 + q)
                j = i * (API // 2) + q // 2
                src = w_ada_v[:, bass.ds(j, 1), col0:col0 + SBW].rearrange("p a n -> p (a n)")
                if not (isinstance(n, int) and n < NA):
                    sp.wait_ge(ada_step, n - (NA - 1))
                sp.dma_start(a_st[:, q % NA, :], src).then_inc(a_landed[q % NA], 16)

            def ada_col(s, q):
                return (D if q % 2 == 1 else 0) + s * SBW

            for q in range(API):
                ada_dma(0, 0, q, ada_col(0, q))
                if q == NA - 1:
                    for n in range(NW):
                        w_in_chunk(0, 0, n // 2, n // 2, n % 2)
                    sp.wait_ge(par_landed, 16 * 10)
                    sp.dma_start(xfull[:], x_v).then_inc(x_landed, 16)
            with sp.Fori(1, NI) as i:
                for q in range(API):
                    ada_dma(0, i, q, ada_col(0, q))

            def step(s, i, last):
                for n in range(2 * TPI):
                    if not (s == 0 and isinstance(i, int) and i == 0 and n < NW):
                        w_in_chunk(s, i, i * TPI + n // 2, n // 2, n % 2)
                    for q in ada_with(n, last):
                        ada_dma((s + 1) * APS, i, q, ada_col(s + 1, q))

            for s in range(NSB - 1):
                step(s, 0, False)
                with sp.Fori(1, NI - 1) as i:
                    step(s, i, False)
                step(s, NI - 1, True)
            s = NSB - 1
            for t in range(NT):
                for half in range(2):
                    n = 2 * t + half
                    w_in_chunk(s, t // TPI, LAST[t], t % TPI, half)
                    for q in gate1_with(n):
                        ada_dma(NSB * APS, q // API, q % API, 2 * D + (q % 2) * SBW)
            for n in range(GOUT // WCH):
                tile, half = n // (GPO // WCH), n % (GPO // WCH)
                wc = NSB * NT * 2 + n
                sp.wait_ge(lo_ready, wc * 2 - 4)
                k0 = (W // P if tile < NCO else 0) + half * WCH * GK
                sp.dma_start(w_st[:, wc % NW, :, :, :].rearrange("p a b n -> p (a b) n"),
                             w_out_v[:, k0:k0 + WCH * GK, (tile % NCO) * CT:(tile % NCO + 1) * CT]).then_inc(w_landed[wc % NW], 16)
                for g in range(NB // 2):
                    if n == gate_wt_with(g):
                        if g == 1:
                            sp.wait_ge(yB_lo_r, NH // 2)
                        if g >= 2:
                            sp.wait_ge(gate_ps, 2 * (g - 1))
                        for k, w in enumerate((lru_wa, lru_wx)):
                            for e in range(2):
                                sp.dma_start(gate_wt[g % 2][:, k, e, :, :],
                                             w[0, e, 2 * g:2 * g + 2, :, :].rearrange("n k j -> k n j")).then_inc(gwt_landed[g % 2], 16)
                for q in gate2_with(n):
                    cn = (NSB + 1) * APS + q
                    sp.wait_ge(ada_step, cn - (NA - 1))
                    j = q % (APS // 2)
                    col = 2 * D + (2 + q // (APS // 2)) * SBW
                    sp.dma_start(a_st[:, cn % NA, :], w_ada_v[:, j, col:col + SBW]).then_inc(a_landed[cn % NA], 16)
            for t in range(NCO):
                sp.wait_ge(fin_dve, t + 1)
                if t < NCO - 1:
                    sp.wait_ge(fin_act, t + 1)
                sp.dma_start(out_v[:, :, t * CT:(t + 1) * CT], out_tile(t)).then_inc(out_stored, 16)
            sp.wait_ge(out_stored, 16 * NCO)

        @block.gpsimd
        def _(pool):
            steps = [0]

            def link(ins):
                steps[0] += 1
                ins.then_inc(pool_step, 1)
                pool.wait_ge(pool_step, steps[0])

            pool.memset(st[:, ST_EPS:ST_EPS + 1], EPS).then_inc(eps_ready, 1)
            link(pool.memset(ident[:], 0.0))
            pool.affine_select(out=ident[:], in_=ident[:], compare_op=ALU.not_equal, fill=1.0, base=0,
                               pattern=[[-1, P]], channel_multiplier=1).then_inc(consts_ready, 1)
            pool.memset(ones[:], 1.0).then_inc(consts_ready, 1)
            pool.memset(maskfill[:], MASK).then_inc(mask_set, 1)

            def scale_xs(s):
                if s == 0:
                    pool.wait_ge(rstd_ready, 1)
                else:
                    pool.wait_ge(xs_landed, 16 * s)
                for tok in range(TOK):
                    src = xfull[:, tok, 0:SBW] if s == 0 else xs[:, tok, :]
                    pool.tensor_scalar(xs[:, tok, :], src, st[:, ST_R + tok:ST_R + tok + 1], None,
                                       ALU.mult).then_inc(xs_scaled, 1)

            scale_xs(0)
            pool.wait_ge(mask_set, 1)
            pool.wait_ge(ada_step, APS)
            pool.dma_start(bias_img.rearrange("c h r k -> (c h r k)").rearrange("(p n) -> p n", p=P),
                           maskfill[:]).then_inc(mask_stored, 16)
            pool.wait_ge(mask_stored, 16)
            img = bias_img
            HALF = WIN_C // 2
            last_c = GW - WIN_C
            n_store = 0
            for ro in range(NRO):
                tab = rpb[0, :, RO0 + ro, :]
                for c0, nc_, tstep, istep, t0, k0 in (
                    (0, HALF, -1, 0, WIN_C - 1, 0),
                    (HALF, last_c + 1, 0, 1, WIN_C - 1 - HALF, 0),
                    (last_c + HALF + 1, HALF - 1, -1, 0, WIN_C - 1 - HALF - 1, last_c),
                ):
                    src = bass.AP(tensor=tab.tensor, offset=tab.offset + t0,
                                  ap=[[tab.ap[0][0], NH], [tstep, nc_], [1, WIN_C]])
                    at = img[c0, 0, ro, k0:k0 + 1]
                    dst = bass.AP(tensor=img.tensor, offset=at.offset,
                                  ap=[[NRO * GW, NH], [NH * NRO * GW + istep, nc_], [1, WIN_C]])
                    pool.dma_start(dst, src).then_inc(img_stored, 16)
                    n_store += 1
            for s in range(1, NSB):
                pool.wait_ge(xT_ps, 4 * s)
                pool.dma_start(xs[:], x_v[:, :, s * SBW:(s + 1) * SBW]).then_inc(xs_landed, 16)
                scale_xs(s)
            pool.wait_ge(mod_ps, NSB)
            pool.memset(mod[:], 0.0).then_inc(gzero, 1)
            pool.wait_ge(gzero, 1)
            pool.dma_start(mod[0:1, :, :].rearrange("p a n -> p (a n)"), b_gate[:, 0:2 * SBW]).then_inc(gbias_landed, 16)
            pool.wait_ge(img_stored, 16 * n_store)
            pool.wait_ge(hl_ready, 4 * NSB)
            for h in range(NH):
                if h >= 2:
                    pool.wait_ge(s_ready, 2 * (h - 1))
                for r in range(ROWS):
                    pool.dma_start(bias[(r % 2) * GW:(r % 2 + 1) * GW, h % 2, r // 2, :].rearrange("p (a n) -> p a n", a=ROWS),
                                   bias_img[:, h, ROWS - 1 - r:2 * ROWS - 1 - r, :]).then_inc(bias_landed[h % 2], 16)
            pool.wait_ge(gran_used, NSB * GSB)
            pool.memset(xaT[:], 0.0).then_inc(pad_set, 1)
            pool.memset(hacc[:], 0.0).then_inc(pad_set, 1)
            pool.wait_ge(pad_set, 2)
            pool.wait_ge(yB_lo_r, NH // 2)
            pool.memset(mod2[:], 0.0).then_inc(gzero, 1)
            pool.wait_ge(gzero, 2)
            pool.dma_start(mod2[0:1, :, :].rearrange("p a n -> p (a n)"), b_gate[:, 2 * SBW:4 * SBW]).then_inc(gbias_landed, 16)
            for g in range(NB // 2):
                for e in range(2):
                    pool.wait_ge(ri_ready, 2 * g + e + 1)
                    pool.tensor_tensor(ib[:, e, :, :], ib[:, e, :, :], xc[:, g % 2, :, :], ALU.mult).then_inc(ixc_ready, 1)
                pool.wait_ge(m_ready, g + 1)
                pool.tensor_scalar(wa_[:], wa_[:], -1.0, 1.0, ALU.mult, ALU.add).then_inc(a_ready, 1)
                pool.wait_ge(y_ready, g + 1)
                pool.tensor_tensor(hh[:], hh[:], hh[:], ALU.mult).then_inc(hsq_ready, 1)
                pool.wait_ge(hsq_ready, g + 1)
                pool.tensor_tensor(hacc[:], hacc[:], hh[:], ALU.add).then_inc(hacc_ready, 1)
                pool.wait_ge(hacc_ready, g + 1)
            pool.wait_ge(yA_lo_r, NB // 2)
            pool.wait_ge(ssA_ps, 1)
            pool.dma_start(fing[:], final_g.rearrange("(a n) -> a n", a=1).to_broadcast([P, D])).then_inc(fing_landed, 16)
            for t in range(2):
                pool.dma_start(xres[:, t, :, :], x_v[:, :, t * CT:(t + 1) * CT]).then_inc(xres_landed[t], 16)
            def times_gate(t):
                pool.wait_ge(gate_ready, t + 1)
                for tok in range(TOK):
                    pool.tensor_tensor(out_tile(t)[:, tok, :], out_tile(t)[:, tok, :], gate_cols(t), ALU.mult).then_inc(pool_step, 1)
                    steps[0] += 1
                pool.wait_ge(pool_step, steps[0])

            def plus_x(t, done):
                pool.wait_ge(xres_landed[t % 2], 16 * (t // 2 + 1))
                pool.tensor_tensor(out_tile(t), out_tile(t), xres[:, t % 2, :, :], ALU.add).then_inc(done, 1)

            for t in range(NCO - 1):
                if t == NCO - 2:
                    pool.wait_ge(evac_B_done, NCO)
                    times_gate(NCO - 1)
                    plus_x(NCO - 1, last_ready)
                pool.wait_ge(evac_done, NSB * NT + t + 1)
                times_gate(t)
                plus_x(t, t3_ready)
                if t + 2 < NCO:
                    pool.wait_ge(t3_ready, t + 1)
                    pool.dma_start(xres[:, t % 2, :, :], x_v[:, :, (t + 2) * CT:(t + 3) * CT]).then_inc(xres_landed[t % 2], 16)
                pool.wait_ge(fss_ready, 2 * t + 2)
                if t == 0:
                    pool.wait_ge(fing_landed, 16)
                for tok in range(TOK):
                    ins = pool.tensor_tensor(out_tile(t)[:, tok, :], out_tile(t)[:, tok, :], fing[:, t * CT:(t + 1) * CT], ALU.mult)
                ins.then_inc(t4_ready, 1)

        @block.scalar
        def _(act):
            steps = [0]

            def link(ins):
                steps[0] += 1
                ins.then_inc(act_step, 1)
                act.wait_ge(act_step, steps[0])

            def dma(dst, src):
                act.dma_start(dst, src).then_inc(par_landed, 16)

            r = par_rows
            dma(r[0:32, 0, :], c.rearrange("b (n p) -> (b n) p", p=P))
            dma(r[32:64, 0, :], norm_g.rearrange("l (n p) -> (l n) p", p=P))
            dma(r[64:128, 0, :], b_ada[:, 0:2 * D].rearrange("l (n p) -> (l n) p", p=P))
            dma(r[0:64, 1, :], conv_w.rearrange("l j (n p) -> (l j n) p", p=P))
            dma(r[64:80, 1, :], conv_b.rearrange("l (n p) -> (l n) p", p=P))
            dma(r[80:96, 1, :], gn_lru.rearrange("l (n p) -> (l n) p", p=P))
            dma(r[96:128, 1, :], lru_ba.rearrange("l e (n p) -> (l e n) p", p=P))
            dma(r[0:32, 2, :], lru_bx.rearrange("l e (n p) -> (l e n) p", p=P))
            dma(r[32:64, 2, :], lru_lambda.rearrange("l e (n p) -> (l e n) p", p=P))
            dma(r[64:80, 2, :], gn_att.rearrange("l (n p) -> (l n) p", p=P))
            act.wait_ge(par_ps, 1)
            act.copy(par[:], side[0][:, 0:NPAR]).then_inc(par_ready, 1)
            act.wait_ge(par_ready, 1)
            act.activation(cond[:], par[:, C_C:C_C + 32], ACT.Sigmoid).then_inc(sigc_ready, 1)
            act.wait_ge(x_landed, 16)
            for tok in range(TOK):
                link(act.activation(xsq[:, tok, :], xfull[:, tok, :], ACT.Square,
                                    accum_out=st[:, ST_SS + tok:ST_SS + tok + 1]))
            act.wait_ge(eps_ready, 1)
            act.activation(st[:, ST_RT:ST_RT + 2], st[:, ST_SS:ST_SS + 2], ACT.Sqrt,
                           bias=st[:, ST_EPS:ST_EPS + 1], scale=1.0 / D).then_inc(xroot_ready, 1)
            act.wait_ge(lam_ready, 1)
            act.activation(tl[:, 1, :], tl[:, 0, :], ACT.Exp, scale=-1.0).then_inc(elam_ready, 1)

            def split_hi(gr, slot_chunk, n_chunk, which, slot_gr, wait_used):
                if which == 0:
                    act.wait_ge(w_landed[slot_chunk], n_chunk)
                if wait_used:
                    act.wait_ge(gran_used, gr - (NG - 1))
                act.copy(w_hi[:, slot_gr, :, :], w_st[:, slot_chunk, which, :, :]).then_inc(hi_ready, 1)

            def split_h(s, g):
                if s > 0:
                    act.wait_ge(gran_used, s * GSB - GPT + g + 1)
                act.wait_ge(h32_ready, 4 * s + g + 1)
                act.copy(h_hi[:, 2 * g:2 * g + 2, :], h32[:, 2 * g:2 * g + 2, :]).then_inc(hh_ready, 1)

            def step(s, i, first):
                for u in range(TPI):
                    for g in range(GPT):
                        n = u * GPT + g
                        if first and s == 0 and n < NG:
                            continue
                        if first and s > 0 and n < 3:
                            for k in ((0, 1), (2,), (3,))[n]:
                                split_h(s, k)
                        c0 = s * NT * 2 + n // 2
                        gr = i * (TPI * GPT) + (s * GSB + n)
                        used = not (isinstance(gr, int) and gr < NG)
                        split_hi(gr, c0 % NW, (i * (2 * TPI // NW) + c0 // NW + 1) * 16, n % 2, n % NG, used)

            for n in range(NG):
                split_hi(n, n // 2, 16, n % 2, n, False)
            for k in range(GPT):
                split_h(0, k)
            for s in range(NSB - 1):
                step(s, 0, True)
                with act.Fori(1, NI) as i:
                    step(s, i, False)

            def copy_qkT(h):
                act.wait_ge(qkT_ps, h + 1)
                if h >= 1:
                    act.wait_ge(s_ps, h)
                act.copy(qkT[:].rearrange("p a n -> p (a n)"), side[2][:]).then_inc(qkT_ready, 1)

            def exps(h):
                act.wait_ge(s_ready, 2 * h + 2)
                for tok in range(TOK):
                    act.activation(prob[:, h % 2, tok, :], prob[:, h % 2, tok, :], ACT.Exp,
                                   bias=mx[:, h % 2, tok:tok + 1], accum_out=es[:, h % 4, tok:tok + 1]).then_inc(p_ready, 1)

            def copy_probT(h):
                act.wait_ge(pT_ps, h + 1)
                if h >= 1:
                    act.wait_ge(o_ps, h)
                act.copy(probT[:].rearrange("p a n -> p (a n)"), side[0][:]).then_inc(pT_ready, 1)

            def scale_o(h):
                act.wait_ge(o_ps, h + 1)
                act.wait_ge(rinv_ready, h + 1)
                for tok in range(TOK):
                    ins = act.activation(head(QB, h, tok), side[1][:, tok * P:(tok + 1) * P], ACT.Copy,
                                         scale=es[:, h % 4, tok:tok + 1])
                ins.then_inc(o_ready, 1)

            def gate_sig(t):
                act.wait_ge(evac_done, (NSB - 1) * NT + LAST.index(GB + t) + 1)
                if t >= 1:
                    act.wait_ge(z_ready, t)
                act.activation(sig[:], proj[:, GB + t, :, :], ACT.Sigmoid).then_inc(sig_ready, 1)

            def squares_B(t):
                act.wait_ge(o_ready, 4 * (t + 1))
                for tok in range(TOK):
                    act.activation(proj[:, VB + t, tok, :], proj[:, QB + t, tok, :], ACT.Square,
                                   accum_out=st[:, ST_BP + 4 * tok + t:ST_BP + 4 * tok + t + 1]).then_inc(ssB_part, 1)

            def norm_B():
                act.wait_ge(ssB_ready, 1)
                act.activation(st[:, ST_BR:ST_BR + 2], st[:, ST_B:ST_B + 2], ACT.Sqrt,
                               bias=st[:, ST_EPS:ST_EPS + 1], scale=1.0 / W).then_inc(rB_ready, 1)

            def yB_upper(r):
                act.wait_ge(yBT_ps, r + 1)
                for k in range(2):
                    n = 2 * r + k
                    ins = act.activation(yB_hi[:, n, :], side[2 + r % 2][:, k * S:(k + 1) * S], ACT.Copy,
                                         scale=par[:, C_GNA + n:C_GNA + n + 1])
                ins.then_inc(yB_hi_r, 1)

            s = NSB - 1
            for g in range(GSB):
                if g < 3:
                    for k in ((0, 1), (2,), (3,))[g]:
                        split_h(s, k)
                for h in range(NH):
                    if g == copy_qkT_at(h):
                        copy_qkT(h)
                    if g == exps_at(h):
                        exps(h)
                    if g == copy_probT_at(h):
                        copy_probT(h)
                    if g == scale_o_at(h):
                        scale_o(h)
                for t in range(NH // 4):
                    if g == squares_B_at(t):
                        squares_B(t)
                if g == NORM_B_AT:
                    norm_B()
                for t in range(NH // 4):
                    if g == gate_at(t):
                        gate_sig(t)
                for r in range(NH // 2):
                    if g == yBT_at(r) + NG:
                        yB_upper(r)
                c0 = s * NT * 2 + g // 2
                split_hi(s * GSB + g, c0 % NW, (c0 // NW + 1) * 16, g % 2, g % NG, True)

            def lru_transposed(g):
                act.wait_ge(xaT_ps, g + 1)
                if g == 0:
                    act.wait_ge(pad_set, 2)
                else:
                    act.wait_ge(xc_ready, g)
                act.copy(xaT[:, :, 2:2 + S], side[0][:].rearrange("p (k n) -> p k n", k=2)).then_inc(xaT_ready, 1)

            def lru_gate_sigmoid(g):
                act.wait_ge(gaT_ps, g + 1)
                if g > 0:
                    act.wait_ge(y_ready, g)
                act.activation(gaS[:], side[2][:].rearrange("p (k n) -> p k n", k=2), ACT.Sigmoid).then_inc(gsig_ready, 1)

            def lru_sigmoids(g, e):
                act.wait_ge(gate_ps, 2 * g + e + 1)
                if g >= 1:
                    act.wait_ge(h_ready, g)
                for k in range(2):
                    n = e * NB + 2 * g + k
                    act.activation(rv[:, e, k, :], side[1][:, k * S:(k + 1) * S], ACT.Sigmoid,
                                   bias=par[:, C_BA + n:C_BA + n + 1]).then_inc(r_ready, 1)
                    ins = act.activation(ib[:, e, k, :], side[3][:, k * S:(k + 1) * S], ACT.Sigmoid,
                                         bias=par[:, C_BX + n:C_BX + n + 1])
                ins.then_inc(ri_ready, 1)

            def lru_decay(g):
                act.wait_ge(r_ready, 4 * g + 4)
                act.wait_ge(coef_ready, 2)
                for e in range(2):
                    for k in range(2):
                        n = e * NB + 2 * g + k
                        act.activation(wa_[:, e, k, :], rv[:, e, k, :], ACT.Exp, scale=coef[:, 1, n:n + 1])
                        ins = act.activation(rv[:, e, k, :], rv[:, e, k, :], ACT.Tanh, scale=coef[:, 0, n:n + 1])
                ins.then_inc(v_ready, 1)

            def lru_root(g):
                act.wait_ge(m_ready, g + 1)
                act.activation(rv[:], rv[:], ACT.Sqrt).then_inc(sq_ready, 1)

            def lru_sigmoid_table():
                act.activation(mx[:, 0, 0:1], st[:, ST_EPS:ST_EPS + 1], ACT.Sigmoid)

            def yA_upper(g):
                act.wait_ge(y_ready, g + 1)
                if g % 2 == 0:
                    act.wait_ge(gaT_ps, g + 2)
                act.copy(yA_hi[:, 2 * g:2 * g + 2, :], yA[:, 2 * g:2 * g + 2, :]).then_inc(yA_hi_r, 1)

            def norm_A():
                act.wait_ge(ssA_ps, 1)
                act.activation(st[:, ST_AR:ST_AR + 2], side[0][:, 0:2], ACT.Sqrt,
                               bias=st[:, ST_EPS:ST_EPS + 1], scale=1.0 / W).then_inc(rA_ready, 1)

            def gate_copy(n):
                act.wait_ge(gate_bc_ps, n + 1)
                m = mod if n < 4 else mod2
                act.copy(m[:, (n % 4) // 2, (n % 2) * CT:(n % 2 + 1) * CT], side[1 + n % 3][:]).then_inc(gate_ready, 1)

            def squares(t):
                if t < NCO - 1:
                    act.wait_ge(t3_ready, t + 1)
                for tok in range(TOK):
                    if t == NCO - 1:
                        act.wait_ge(sum_ready, tok + 1)
                    if t + tok > 0:
                        act.wait_ge(fss_ready, 2 * t + tok)
                    act.activation(side[0][:], out_tile(t)[:, tok, :], ACT.Square,
                                   accum_out=fss[:, tok, t:t + 1]).then_inc(fss_ready, 1)

            def evac_B(o):
                act.wait_ge(gran_used, NSB * GSB + (o + 1) * GPO)
                if o == 0:
                    act.wait_ge(rB_inv, 1)
                for tok in range(TOK):
                    ins = act.activation(out_tile(o)[:, tok, :], acc[o % 2][tok][:], ACT.Copy,
                                         scale=st[:, ST_BR + tok:ST_BR + tok + 1])
                ins.then_inc(evac_B_done, 1)

            for g in range(GOUT):
                for n in range(NCO):
                    if g == evac_at(n):
                        evac_B(n)
                for n in range(NB // 2):
                    k = g - LRU_STEP * n
                    if k == 4:
                        lru_transposed(n)
                    if k == LRU_GA + 4:
                        lru_gate_sigmoid(n)
                    if k in (LRU_G0 + 5, LRU_G1 + 4):
                        lru_sigmoids(n, int(k > LRU_G0 + 5))
                    if k == LRU_G1 + 5:
                        lru_decay(n)
                    if k == LRU_G1 + 6:
                        lru_root(n)
                    if k == LRU_G1 + 7 and n < NB // 2 - 1:
                        lru_sigmoid_table()
                    if k == LRU_Y + 3:
                        yA_upper(n)
                if g == NORM_A_AT + 3:
                    norm_A()
                for n in range(NCO):
                    if g == gate_bc_at(n) + 3:
                        gate_copy(n)
                    if g == evac_at(NCO + n) + 3:
                        squares(n)
                wc = NSB * NT * 2 + g // 2
                split_hi(NSB * GSB + g, wc % NW, (wc // NW + 1) * 16, g % 2, g % NG, True)
            squares(NCO - 1)
            act.wait_ge(fsum_ready, 1)
            act.activation(st[:, ST_FR:ST_FR + 2], st[:, ST_F:ST_F + 2], ACT.Sqrt,
                           bias=st[:, ST_EPS:ST_EPS + 1], scale=1.0 / D).then_inc(rF_ready, 1)
            act.wait_ge(rF_inv, 1)
            for t in range(NCO - 1):
                act.wait_ge(t4_ready, t + 1)
                act.activation(out_tile(t)[:, 1, :], out_tile(t)[:, 1, :], ACT.Copy,
                               scale=st[:, ST_FR + 1:ST_FR + 2]).then_inc(fin_act, 1)

        @block.vector
        def _(dve):
            steps = [0]

            def link(ins):
                steps[0] += 1
                ins.then_inc(dve_step, 1)
                dve.wait_ge(dve_step, steps[0])

            dve.wait_ge(sigc_ready, 1)
            dve.tensor_tensor(cond[:], cond[:], par[:, C_C:C_C + 32], ALU.mult).then_inc(cond_ready, 1)
            dve.wait_ge(cond_ready, 1)
            lam = par[:, C_LAM:C_LAM + 32]
            dve.scalar_tensor_tensor(out=tl[:, 0, :], in0=lam, scalar=-1.0, in1=lam, op0=ALU.mult, op1=ALU.max).then_inc(lam_ready, 1)

            def ada(n, slot, n_land, acc_t, which, cnd, first, back):
                dve.wait_ge(a_landed[slot], n_land)
                if first:
                    dve.tensor_scalar(acc_t[:, which, :], a_st[:, slot, :], cnd, None, ALU.mult).then_inc(ada_step, 1)
                    return
                dve.wait_ge(ada_step, n - (back - 1))
                dve.scalar_tensor_tensor(out=acc_t[:, which, :], in0=a_st[:, slot, :], scalar=cnd,
                                         in1=acc_t[:, which, :], op0=ALU.mult, op1=ALU.add).then_inc(ada_step, 1)

            def ada_in(s, i, q):
                n = i * API + (s * APS + q)
                j = i * (API // 2) + q // 2
                first = isinstance(i, int) and i == 0 and q < 2
                if first and s > 0:
                    dve.wait_ge(mod_ps, s)
                cnd = cond[:, j:j + 1] if isinstance(j, int) else cond[:, bass.ds(j, 1)]
                ada(n, q % NA, (i * (API // NA) + ((s * APS + q) // NA + 1)) * 16, mod, 1 - q % 2, cnd, first, 2)

            def split_lo(gr, slot_chunk, which, slot_gr):
                dve.wait_ge(hi_ready, gr + 1)
                dve.tensor_tensor(w_lo[:, slot_gr, :, :], w_st[:, slot_chunk, which, :, :],
                                  w_hi[:, slot_gr, :, :].bitcast(F32), ALU.subtract).then_inc(lo_ready, 1)

            def split_h(s, g):
                dve.wait_ge(hh_ready, 4 * s + g + 1)
                dve.tensor_tensor(h_lo[:, 2 * g:2 * g + 2, :], h32[:, 2 * g:2 * g + 2, :],
                                  h_hi[:, 2 * g:2 * g + 2, :].bitcast(F32), ALU.subtract).then_inc(hl_ready, 1)

            def evac(s, t, tile, buf):
                n = t + s * NT
                dve.wait_ge(gran_used, n * GPT + GPT)
                if s > 0:
                    dve.wait_ge(evac_done, n - (NT - 1) if s < NSB - 1 else NT * (NSB - 1))
                for tok in range(TOK):
                    if s == 0:
                        ins = dve.tensor_copy(proj_at(tile, tok), acc[buf][tok][:])
                    else:
                        ins = dve.tensor_tensor(proj_at(tile, tok), proj_at(tile, tok), acc[buf][tok][:], ALU.add)
                ins.then_inc(evac_done, 1)

            def mod_columns(s):
                dve.wait_ge(mod_ps, s + 1)
                b0 = s * KT
                link(dve.tensor_tensor(mcols[:, 2, :], side[0][:, 0:KT], par[:, C_BSC + b0:C_BSC + b0 + KT], ALU.add))
                dve.tensor_tensor(mcols[:, 1, :], side[0][:, KT:2 * KT], par[:, C_BSH + b0:C_BSH + b0 + KT], ALU.add).then_inc(mod_cols, 1)
                dve.scalar_tensor_tensor(out=mcols[:, 0, :], in0=mcols[:, 2, :], scalar=1.0,
                                         in1=par[:, C_NG + b0:C_NG + b0 + KT], op0=ALU.add, op1=ALU.mult).then_inc(mod_cols, 1)
                dve.wait_ge(mod_cols, 2 * s + 2)

            def modulate(s, r):
                dve.wait_ge(xT_ps, 4 * s + r + 1)
                if r == 0 and s > 0:
                    dve.wait_ge(hl_ready, 4 * s)
                for k in range(2):
                    n = 2 * r + k
                    ins = dve.tensor_scalar(h32[:, n, :], xT_bank(s, r)[:, k * S:(k + 1) * S],
                                            mcols[:, 0, n:n + 1], mcols[:, 1, n:n + 1], ALU.mult, ALU.add)
                ins.then_inc(h32_ready, 1)

            for q in range(API):
                ada_in(0, 0, q)
            with dve.Fori(1, NI // 2) as i:
                for q in range(API):
                    ada_in(0, i, q)
            dve.wait_ge(xroot_ready, 1)
            dve.reciprocal(st[:, ST_R:ST_R + 2], st[:, ST_RT:ST_RT + 2]).then_inc(rstd_ready, 1)
            with dve.Fori(NI // 2, NI) as i:
                for q in range(API):
                    ada_in(0, i, q)
            for n in range(NG):
                split_lo(n, n // 2, n % 2, n)
            mod_columns(0)
            modulate(0, 0)
            for r in range(1, 4):
                modulate(0, r)
                split_h(0, r - 1)
            split_h(0, 3)
            y, sr, s2, pl = (tl[:, k, :] for k in (1, 2, 3, 4))

            def softplus(part):
                if part == 0:
                    dve.wait_ge(elam_ready, 1)
                    link(dve.tensor_scalar(sr, y, 2.0, None, ALU.add))
                    link(dve.reciprocal(sr, sr))
                    link(dve.tensor_tensor(sr, sr, y, ALU.mult))
                    link(dve.tensor_tensor(s2, sr, sr, ALU.mult))
                    link(dve.tensor_scalar(pl, s2, 1.0 / 19, None, ALU.mult))
                for k in ((17, 15), (13, 11, 9), (7, 5, 3))[part]:
                    link(dve.scalar_tensor_tensor(out=pl, in0=pl, scalar=1.0 / k, in1=s2, op0=ALU.add, op1=ALU.mult))
                if part == 2:
                    link(dve.scalar_tensor_tensor(out=pl, in0=pl, scalar=1.0, in1=sr, op0=ALU.add, op1=ALU.mult))
                    link(dve.tensor_scalar(s2, lam, -1.0, 0.0, ALU.mult, ALU.max))
                    link(dve.scalar_tensor_tensor(out=pl, in0=pl, scalar=2.0, in1=s2, op0=ALU.mult, op1=ALU.add))
                    dve.tensor_scalar(coef[:, 0, :], pl, C_RG / 2, None, ALU.mult).then_inc(coef_ready, 1)
                    dve.tensor_scalar(coef[:, 1, :], pl, -C_RG, None, ALU.mult).then_inc(coef_ready, 1)

            def step(s, i, first, last):
                for u in range(TPI):
                    for g in range(GPT):
                        n = u * GPT + g
                        if first and n == 1 and s > 0:
                            modulate(s, 3)
                        if first and s > 0 and n < 3:
                            for k in ((0, 1), (2,), (3,))[n]:
                                split_h(s, k)
                        for q in half_of(ada_with(n // 2, last), g % 2):
                            ada_in(s + 1, i, q)
                        if last and n == 7:
                            mod_columns(s + 1)
                            modulate(s + 1, 0)
                        if last and n in (10, 11):
                            modulate(s + 1, n - 9)
                        if first and s == 0 and n in (5, 8, 11):
                            softplus((n - 5) // 3)
                        c0 = s * NT * 2 + n // 2
                        if not (first and s == 0 and n < NG):
                            split_lo(i * (TPI * GPT) + (s * GSB + n), c0 % NW, n % 2, n % NG)
                    if first and u == 0:
                        if s == 0:
                            dve.wait_ge(rstd_ready, 1)
                            dve.wait_ge(mask_stored, 16)
                        else:
                            evac(s - 1, NT - 1, NT - 1, (NT - 1) % 3)
                    else:
                        evac(s, i * TPI + (u - 1), i * TPI + (u - 1), (u - 1) % 3)

            for s in range(NSB - 1):
                step(s, 0, True, False)
                with dve.Fori(1, NI - 1) as i:
                    step(s, i, False, False)
                step(s, NI - 1, False, True)

            def add_bias(h):
                dve.wait_ge(s_ps, h + 1)
                dve.wait_ge(bias_landed[h % 2], 16 * ROWS * (h // 2 + 1))
                if h >= 2:
                    dve.wait_ge(pT_ps, h - 1)
                dve.scalar_tensor_tensor(out=prob[:, h % 2, :, :], in0=side[3][:].rearrange("p (t n) -> p t n", t=TOK),
                                         scalar=SCALE, in1=bias[:, h % 2, :, :], op0=ALU.mult, op1=ALU.add).then_inc(s_ready, 1)
                dve.wait_ge(s_ready, 2 * h + 1)
                link(dve.tensor_reduce(mx[:, h % 2, :], prob[:, h % 2, :, :], AX, ALU.max))
                dve.tensor_scalar(mx[:, h % 2, :], mx[:, h % 2, :], -1.0, None, ALU.mult).then_inc(s_ready, 1)

            def rinv(h):
                dve.wait_ge(p_ready, 2 * h + 2)
                dve.reciprocal(es[:, h % 4, :], es[:, h % 4, :]).then_inc(rinv_ready, 1)

            def gate_z(t):
                dve.wait_ge(sig_ready, t + 1)
                link(dve.tensor_tensor(sig[:], sig[:], proj[:, GB + t, :, :], ALU.mult))
                dve.tensor_tensor(proj[:, GB + t, :, :], sig[:], proj[:, QB + t, :, :], ALU.mult).then_inc(z_ready, 1)

            def yB_lower(r):
                dve.wait_ge(yB_hi_r, r + 1)
                for k in range(2):
                    n = 2 * r + k
                    ins = dve.scalar_tensor_tensor(out=yB_lo[:, n, :], in0=side[2 + r % 2][:, k * S:(k + 1) * S],
                                                   scalar=par[:, C_GNA + n:C_GNA + n + 1],
                                                   in1=yB_hi[:, n, :].bitcast(F32), op0=ALU.mult, op1=ALU.subtract)
                ins.then_inc(yB_lo_r, 1)

            s = NSB - 1
            for g in range(GSB):
                t = g // GPT
                if g == 1:
                    modulate(s, 3)
                if g < 3:
                    for k in ((0, 1), (2,), (3,))[g]:
                        split_h(s, k)
                for q in half_of(gate1_with(g // 2), g % 2):
                    if q < 2:
                        dve.wait_ge(gbias_landed, 16)
                    ada(NSB * APS + q, q % NA, ((NSB * APS + q) // NA + 1) * 16, mod, q % 2, cond[:, q // 2:q // 2 + 1], False, 2)
                for h in range(NH):
                    if g == add_bias_at(h):
                        add_bias(h)
                    if g == rinv_at(h):
                        rinv(h)
                for k in range(NH // 4):
                    if g == gate_at(k):
                        gate_z(k)
                if g == squares_B_at(NH // 4 - 1) + 1:
                    dve.wait_ge(ssB_part, TOK * NH // 4)
                    dve.tensor_reduce(st[:, ST_B:ST_B + 2], st[:, ST_BP:ST_BP + 8].rearrange("p (k t) -> p k t", k=TOK),
                                      AX, ALU.add).then_inc(ssB_ready, 1)
                if g == NORM_B_AT + 1:
                    dve.wait_ge(rB_ready, 1)
                    dve.reciprocal(st[:, ST_BR:ST_BR + 2], st[:, ST_BR:ST_BR + 2]).then_inc(rB_inv, 1)
                for r in range(NH // 2):
                    if g == yBT_at(r) + NG:
                        yB_lower(r)
                c0 = s * NT * 2 + g // 2
                split_lo(s * GSB + g, c0 % NW, g % 2, g % NG)
                if g % GPT == GPT - 1:
                    if t == 0:
                        evac(s - 1, NT - 1, NT - 1, (NT - 1) % 3)
                    else:
                        evac(s, t - 1, LAST[t - 1], (t - 1) % 2)

            def convolve(g, k):
                dve.wait_ge(xaT_ready, g + 1)
                if g >= 2:
                    dve.wait_ge(ixc_ready, 2 * g - 2)
                b = 2 * g + k
                for j in range(CONV_W):
                    n = C_CW + j * NB + b
                    src = xaT[:, k, j:j + S]
                    if j == 0:
                        ins = dve.tensor_scalar(xc[:, g % 2, k, :], src, par[:, n:n + 1], par[:, C_CB + b:C_CB + b + 1],
                                                ALU.mult, ALU.add)
                    else:
                        ins = dve.scalar_tensor_tensor(out=xc[:, g % 2, k, :], in0=src, scalar=par[:, n:n + 1],
                                                       in1=xc[:, g % 2, k, :], op0=ALU.mult, op1=ALU.add)
                    if j < CONV_W - 1:
                        link(ins)
                if k == 1:
                    ins.then_inc(xc_ready, 1)

            def gate_silu(g):
                dve.wait_ge(gsig_ready, g + 1)
                dve.tensor_tensor(gaS[:], gaS[:], side[2][:].rearrange("p (k n) -> p k n", k=2), ALU.mult).then_inc(gaS_ready, 1)

            def flat(t):
                return t[:].rearrange("p e k n -> p (e k n)")

            def decay(g):
                dve.wait_ge(v_ready, g + 1)
                dve.wait_ge(ixc_ready, 2 * g + 2)
                dve.scalar_tensor_tensor(out=flat(ib), in0=flat(wa_), scalar=1.0, in1=flat(ib), op0=ALU.add,
                                         op1=ALU.mult).then_inc(b_ready, 1)
                dve.scalar_tensor_tensor(out=flat(wa_), in0=flat(wa_), scalar=1.0, in1=flat(rv), op0=ALU.add,
                                         op1=ALU.mult).then_inc(m_ready, 1)

            def inputs(g):
                dve.wait_ge(sq_ready, g + 1)
                dve.wait_ge(b_ready, 2 * g + 1)
                dve.tensor_tensor(ib[:], ib[:], rv[:], ALU.mult).then_inc(b_ready, 1)

            def scans(g):
                dve.wait_ge(b_ready, 2 * g + 2)
                dve.wait_ge(a_ready, g + 1)
                for k in range(2):
                    dve.tensor_tensor_scan(rv[:, 0, k, :], wa_[:, 0, k, :], ib[:, 0, k, :], 0.0, ALU.mult, ALU.add).then_inc(scan_ready, 1)
                    dve.tensor_tensor_scan(rv[:, 1, k, ::-1], wa_[:, 1, k, ::-1], ib[:, 1, k, ::-1], 0.0,
                                           ALU.mult, ALU.add).then_inc(scan_ready, 1)
                dve.wait_ge(scan_ready, 4 * g + 4)
                if g >= 1:
                    dve.wait_ge(hacc_ready, g)
                dve.tensor_tensor(hh[:], rv[:, 0, :, :], rv[:, 1, :, :], ALU.add).then_inc(h_ready, 1)

            def gated(g):
                dve.wait_ge(h_ready, g + 1)
                dve.wait_ge(gaS_ready, g + 1)
                if g % 2 == 0:
                    dve.wait_ge(xaT_ps, g + 2)
                for k in range(2):
                    b = 2 * g + k
                    ins = dve.scalar_tensor_tensor(out=yA[:, b, :], in0=hh[:, k, :],
                                                   scalar=par[:, C_GNL + b:C_GNL + b + 1], in1=gaS[:, k, :],
                                                   op0=ALU.mult, op1=ALU.mult)
                ins.then_inc(y_ready, 1)

            def yA_lower(g):
                dve.wait_ge(yA_hi_r, g + 1)
                dve.tensor_tensor(yA_lo[:, 2 * g:2 * g + 2, :], yA[:, 2 * g:2 * g + 2, :],
                                  yA_hi[:, 2 * g:2 * g + 2, :].bitcast(F32), ALU.subtract).then_inc(yA_lo_r, 1)

            def evac_out(o):
                n = NSB * GSB + (o + 1) * GPO
                dve.wait_ge(gran_used, n)
                t = out_tile(o % NCO)
                if o == NCO:
                    dve.wait_ge(rA_ready, 1)
                    link(dve.reciprocal(st[:, ST_AR:ST_AR + 2], st[:, ST_AR:ST_AR + 2]))
                    dve.wait_ge(evac_B_done, NCO)
                for tok in range(TOK):
                    ins = dve.scalar_tensor_tensor(out=t[:, tok, :], in0=acc[o % 2][tok][:],
                                                   scalar=st[:, ST_AR + tok:ST_AR + tok + 1], in1=t[:, tok, :],
                                                   op0=ALU.mult, op1=ALU.add)
                ins.then_inc(evac_done, 1)

            for g in range(GOUT):
                for n in range(NB // 2):
                    k = g - LRU_STEP * n
                    if k in (4, 5):
                        convolve(n, k - 4)
                    if k == LRU_GA + 4:
                        gate_silu(n)
                    if k == LRU_G1 + 5:
                        decay(n)
                    if k == LRU_G1 + 6:
                        inputs(n)
                    if k == LRU_Y:
                        scans(n)
                        gated(n)
                    if k == LRU_Y + 3:
                        yA_lower(n)
                split_lo(NSB * GSB + g, (NSB * NT * 2 + g // 2) % NW, g % 2, g % NG)
                for q in half_of(gate2_with(g // 2), g % 2):
                    if q == 0:
                        dve.wait_ge(gbias_landed, 32)
                    cn, j = (NSB + 1) * APS + q, q % (APS // 2)
                    ada(cn, cn % NA, (cn // NA + 1) * 16, mod2, q // (APS // 2), cond[:, j:j + 1], False, 1)
                if g == GPT - 1:
                    evac(NSB - 1, NT - 1, LAST[NT - 1], (NT - 1) % 2)
                for o in range(2 * NCO - 1):
                    if o >= NCO and g == evac_at(o):
                        evac_out(o)
            t = NCO - 1
            dve.wait_ge(gran_used, NSB * GSB + GOUT)
            dve.wait_ge(last_ready, 1)
            dve.wait_ge(gate_ready, NCO)
            for tok in range(TOK):
                link(dve.scalar_tensor_tensor(out=xres[:, t % 2, tok, :], in0=acc[t % 2][tok][:], scalar=st[:, ST_AR + tok:ST_AR + tok + 1],
                                              in1=gate_cols(t), op0=ALU.mult, op1=ALU.mult))
                dve.tensor_tensor(out_tile(t)[:, tok, :], out_tile(t)[:, tok, :], xres[:, t % 2, tok, :], ALU.add).then_inc(sum_ready, 1)
            dve.wait_ge(fss_ready, 2 * NCO)
            dve.tensor_reduce(st[:, ST_F:ST_F + 2], fss[:], AX, ALU.add).then_inc(fsum_ready, 1)
            dve.wait_ge(rF_ready, 1)
            dve.reciprocal(st[:, ST_FR:ST_FR + 2], st[:, ST_FR:ST_FR + 2]).then_inc(rF_inv, 1)
            dve.wait_ge(rF_inv, 1)
            for t in range(NCO - 1):
                dve.wait_ge(t4_ready, t + 1)
                dve.tensor_scalar(out_tile(t)[:, 0, :], out_tile(t)[:, 0, :], st[:, ST_FR:ST_FR + 1], None, ALU.mult).then_inc(fin_dve, 1)
            t = NCO - 1
            for tok in range(TOK):
                ins = dve.scalar_tensor_tensor(out=out_tile(t)[:, tok, :], in0=out_tile(t)[:, tok, :],
                                               scalar=st[:, ST_FR + tok:ST_FR + tok + 1], in1=fing[:, t * CT:(t + 1) * CT],
                                               op0=ALU.mult, op1=ALU.mult)
            ins.then_inc(fin_dve, 1)

        @block.tensor
        def _(pe):
            pe.wait_ge(consts_ready, 2)
            pe.wait_ge(par_landed, 16 * 10)
            pe.transpose(side[0][:, 0:P], par_rows[:, 0, :], ident[:])
            pe.transpose(side[0][:, P:2 * P], par_rows[:, 1, :], ident[:])
            pe.transpose(side[0][:, 2 * P:NPAR], par_rows[0:NPAR - 2 * P, 2, :],
                         ident[0:NPAR - 2 * P, 0:NPAR - 2 * P]).then_inc(par_ps, 1)

            def granule(slot, up, low, k0, buf, first, last, gr):
                pe.wait_ge(lo_ready, gr + 1)
                for k in range(GK):
                    for tok in range(TOK):
                        lh = up[:, k0 + k, tok * P:(tok + 1) * P]
                        ll = low[:, k0 + k, tok * P:(tok + 1) * P]
                        pe.matmul(acc[buf][tok][:], lh, w_hi[:, slot, k, :], start=first and k == 0, stop=False)
                        pe.matmul(acc[buf][tok][:], lh, w_lo[:, slot, k, :], start=False, stop=False)
                        ins = pe.matmul(acc[buf][tok][:], ll, w_hi[:, slot, k, :], start=False, stop=last and k == GK - 1)
                ins.then_inc(gran_used, 1)

            def mod_sums(s):
                pe.wait_ge(ada_step, APS * (s + 1))
                if s == 0:
                    pe.wait_ge(par_ready, 1)
                else:
                    pe.wait_ge(h32_ready, 4 * s)
                for k in range(2 * KT):
                    ins = pe.matmul(side[0][:, k:k + 1], mod[:, k // KT, (k % KT) * P:(k % KT + 1) * P], ones[:, 0:1],
                                    start=True, stop=True)
                ins.then_inc(mod_ps, 1)

            def transpose_x(s, r):
                pe.wait_ge(xs_scaled, 2 * (s + 1))
                if r == 1 and s > 0:
                    pe.wait_ge(mod_cols, 2 * s + 2)
                if r >= 2 and s > 0:
                    pe.wait_ge(h32_ready, 4 * s + r - 1)
                for k in range(2):
                    for tok in range(TOK):
                        ins = pe.transpose(xT_bank(s, r)[:, k * S + tok * P:k * S + (tok + 1) * P],
                                           xs[:, tok, (2 * r + k) * P:(2 * r + k + 1) * P], ident[:])
                ins.then_inc(xT_ps, 1)

            for r in range(4):
                transpose_x(0, r)
            mod_sums(0)

            def step(s, i, first, last):
                for u in range(TPI):
                    n = i * TPI + (s * NT + u)
                    if not (isinstance(n, int) and n < 3):
                        pe.wait_ge(evac_done, n - 2)
                    for g in range(GPT):
                        if first and u == 0:
                            pe.wait_ge(hl_ready, 4 * s + g + 1)
                        n = u * GPT + g
                        if last and n == 4:
                            mod_sums(s + 1)
                            transpose_x(s + 1, 0)
                        if last and n in (7, 8, 10):
                            transpose_x(s + 1, (7, 8, 10).index(n) + 1)
                        gr = i * (TPI * GPT) + (s * GSB + n)
                        granule((u * GPT + g) % NG, h_hi, h_lo, GK * g, u, g == 0, g == GPT - 1, gr)

            for s in range(NSB - 1):
                step(s, 0, True, False)
                with pe.Fori(1, NI - 1) as i:
                    step(s, i, False, False)
                step(s, NI - 1, False, True)

            def transpose_qk(h):
                if h == 0:
                    pe.wait_ge(hl_ready, 4 * NSB)
                tile = 3 * (h // 4) + 2
                pe.wait_ge(evac_done, (NSB - 1) * NT + tile + 1)
                if h >= 1:
                    pe.wait_ge(qkT_ready, h)
                for a, part in enumerate((QB, KB)):
                    for tok in range(TOK):
                        ins = pe.transpose(side[2][:, a * S + tok * P:a * S + (tok + 1) * P], head(part, h, tok), ident[:])
                ins.then_inc(qkT_ps, 1)

            def scores(h):
                pe.wait_ge(qkT_ready, h + 1)
                if h >= 1:
                    pe.wait_ge(s_ready, 2 * h - 1)
                for tok in range(TOK):
                    ins = pe.matmul(side[3][:, tok * S:(tok + 1) * S], qkT[:, 0, tok * P:(tok + 1) * P], qkT[:, 1, :],
                                    start=True, stop=True)
                ins.then_inc(s_ps, 1)

            def transpose_p(h):
                pe.wait_ge(p_ready, 2 * h + 2)
                if h >= 1:
                    pe.wait_ge(pT_ready, h)
                for kt in range(2):
                    for tok in range(TOK):
                        ins = pe.transpose(side[0][:, kt * S + tok * P:kt * S + (tok + 1) * P],
                                           prob[:, h % 2, tok, kt * P:(kt + 1) * P], ident[:])
                ins.then_inc(pT_ps, 1)

            def p_times_v(h):
                pe.wait_ge(pT_ready, h + 1)
                if h >= 1:
                    pe.wait_ge(o_ready, h)
                for tok in range(TOK):
                    for kt in range(2):
                        ins = pe.matmul(side[1][:, tok * P:(tok + 1) * P], probT[:, kt, tok * P:(tok + 1) * P],
                                        head(VB, h, kt), start=(kt == 0), stop=(kt == 1))
                ins.then_inc(o_ps, 1)

            def transpose_yB(r):
                pe.wait_ge(z_ready, r // 2 + 1)
                if r == 0:
                    pe.wait_ge(s_ready, 2 * NH)
                if r >= 2:
                    pe.wait_ge(yB_lo_r, r - 1)
                for k in range(2):
                    for tok in range(TOK):
                        ins = pe.transpose(side[2 + r % 2][:, k * S + tok * P:k * S + (tok + 1) * P],
                                           head(GB, 2 * r + k, tok), ident[:])
                ins.then_inc(yBT_ps, 1)

            s = NSB - 1
            for g in range(GSB):
                t = g // GPT
                for h in range(NH):
                    if g == qk_at(h):
                        transpose_qk(h)
                    if g == scores_at(h):
                        scores(h)
                    if g == pT_at(h):
                        transpose_p(h)
                    if g == pv_at(h):
                        p_times_v(h)
                for r in range(NH // 2):
                    if g == yBT_at(r):
                        transpose_yB(r)
                if g % GPT == 0:
                    pe.wait_ge(evac_done, s * NT + t - 1)
                if g < GPT:
                    pe.wait_ge(hl_ready, 4 * s + g + 1)
                granule(g % NG, h_hi, h_lo, GK * (g % GPT), t % 2, g % GPT == 0, g % GPT == GPT - 1, s * GSB + g)

            def transpose_lru(g, part, bank, done):
                if g == 0:
                    pe.wait_ge(evac_done, (NSB - 1) * NT + NT - 1 if part == XB else NSB * NT)
                    pe.wait_ge(yB_lo_r, NH // 2)
                    pe.wait_ge(o_ready, NH)
                elif part == XB:
                    pe.wait_ge(xaT_ready, g)
                else:
                    pe.wait_ge(gaS_ready, g)
                for k in range(2):
                    for tok in range(TOK):
                        b = (2 * g + k) % 4
                        ins = pe.transpose(side[bank][:, k * S + tok * P:k * S + (tok + 1) * P],
                                           proj[:, part + g // 2, tok, b * P:(b + 1) * P], ident[:])
                ins.then_inc(done, 1)

            def lru_gates(g, e):
                pe.wait_ge(xc_ready, g + 1)
                pe.wait_ge(gwt_landed[g % 2], 64 * (g // 2 + 1))
                if g + e > 0:
                    pe.wait_ge(ri_ready, 2 * g + e)
                for k in range(2):
                    bank = side[(1, 3)[k]]
                    for n in range(2):
                        ins = pe.matmul(bank[:, n * S:(n + 1) * S], gate_wt[g % 2][:, k, e, n, :], xc[:, g % 2, n, :],
                                        start=True, stop=True)
                ins.then_inc(gate_ps, 1)

            def sum_squares_A():
                pe.wait_ge(hacc_ready, NB // 2)
                pe.wait_ge(xaT_ready, NB // 2)
                for tok in range(TOK):
                    for k in range(2):
                        ins = pe.matmul(side[0][:, tok:tok + 1], hacc[:, k, tok * P:(tok + 1) * P], ones[:, 0:1],
                                        start=(k == 0), stop=(k == 1))
                ins.then_inc(ssA_ps, 1)

            def gate_broadcast(n):
                if n == 0:
                    pe.wait_ge(ada_step, (NSB + 1) * APS)
                    pe.wait_ge(ri_ready, NB)
                    pe.wait_ge(gaS_ready, NB // 2)
                if n == 4:
                    pe.wait_ge(ada_step, (NSB + 1) * APS + APS // 2)
                if n == 6:
                    pe.wait_ge(ada_step, (NSB + 2) * APS)
                if n >= 3:
                    pe.wait_ge(gate_ready, n - 2)
                m = mod if n < 4 else mod2
                pe.matmul(side[1 + n % 3][:], ones[:], m[:, (n % 4) // 2, (n % 2) * CT:(n % 2 + 1) * CT],
                          start=True, stop=True).then_inc(gate_bc_ps, 1)

            for g in range(GOUT):
                for n in range(NB // 2):
                    k = g - LRU_STEP * n
                    if k == 0:
                        transpose_lru(n, XB, 0, xaT_ps)
                    if k == LRU_GA:
                        transpose_lru(n, GA, 2, gaT_ps)
                    if k in (LRU_G0, LRU_G1):
                        lru_gates(n, int(k > LRU_G0))
                if g == NORM_A_AT:
                    sum_squares_A()
                for n in range(NCO):
                    if g == gate_bc_at(n):
                        gate_broadcast(n)
                o, k = g // GPO, g % GPO
                if k == 0:
                    if 2 <= o < NCO + 2:
                        pe.wait_ge(evac_B_done, o - 1)
                    else:
                        pe.wait_ge(evac_done, NSB * NT - 1 + (o if o < 2 else o - NCO))
                if o == 0:
                    pe.wait_ge(yB_lo_r, k + 1)
                if o == NCO:
                    pe.wait_ge(yA_lo_r, k + 1)
                up, low = (yB_hi, yB_lo) if o < NCO else (yA_hi, yA_lo)
                granule(g % NG, up, low, GK * k, o % 2, k == 0, k == GPO - 1, NSB * GSB + g)


def qk_at(h): return 3 * h + 17
def copy_qkT_at(h): return qk_at(h) + 3
def scores_at(h): return qk_at(h) + 5
def add_bias_at(h): return scores_at(h) + 3
def exps_at(h): return add_bias_at(h) + 1
def pT_at(h): return exps_at(h) + 2
def copy_probT_at(h): return pT_at(h) + 3
def pv_at(h): return copy_probT_at(h) + 1
def rinv_at(h): return pv_at(h) + 1
def scale_o_at(h): return pv_at(h) + 3


def squares_B_at(t): return scale_o_at(4 * t + 3) + 1
def gate_at(t): return scale_o_at(4 * t + 3) + (14, 8, 3, 2)[t]
def yBT_at(r): return gate_at(2) + 1 + 2 * r if r < 6 else gate_at(3) + 2 * (r - 5)


NORM_B_AT = yBT_at(NH // 2 - 1) + NG
LRU_STEP = 7
LRU_G0, LRU_G1 = 5, 9
LRU_GA = 7
LRU_Y = LRU_G1 + 7
NORM_A_AT = (NB // 2 - 1) * LRU_STEP + LRU_Y + 4


def evac_at(o): return (o + 1) * GPO + 3
def gate_bc_at(n): return NCO * GPO + (10 + n if n < 4 else 41 + (n - 4) if n < 6 else 54 + (n - 6))


def ada_with(n, last):
    share = (3, 3, 2, 0, 0, 0) if last else (2, 1, 1, 2, 1, 1)
    return list(range(sum(share[:n]), sum(share[:n + 1])))


def half_of(chunks, second):
    cut = (len(chunks) + 1) // 2
    return chunks[cut:] if second else chunks[:cut]


def gate1_with(n):
    return list(range(4 * n // 3, min(4 * (n + 1) // 3, APS)))


def gate_wt_with(g):
    return 3 * g if g < 2 else (LRU_STEP * (g - 2) + LRU_G1 + 12) // 2


def gate2_with(n):
    half = GOUT // WCH // 2
    at = [min(APS, max(0, k - 3) * 28 // (half - 3) if k < half else 28 + (k - half) * (APS - 28) // (half - 6))
          for k in (n, n + 1)]
    return list(range(*at))


_OUT = ((1, S, D), 'float32')
_NAMES = ['x', 'c', 'norm_g', 'w_ada', 'b_ada', 'w_in', 'conv_w', 'conv_b', 'lru_wa', 'lru_ba', 'lru_wx', 'lru_bx',
          'lru_lambda', 'rpb', 'gn_lru', 'gn_att', 'w_out', 'final_g']


def kernel(**inputs):
    import numpy as np
    import concourse.bacc as bacc
    from concourse.bass_utils import run_bass_kernel_spmd

    nc = bacc.Bacc("TRN2", target_bir_lowering=False, num_devices=1)
    arrays, args = {}, []
    for name in _NAMES:
        a = np.ascontiguousarray(inputs[name])
        arrays[f"in_{name}"] = a
        args.append(nc.dram_tensor(f"in_{name}", a.shape, mybir.dt.from_np(a.dtype), kind="ExternalInput").ap())
    out = nc.dram_tensor("out_0", _OUT[0], F32, kind="ExternalOutput").ap()
    build(nc, *args, out)
    r = run_bass_kernel_spmd(nc, [arrays], core_ids=[0])
    return r.results[0]["out_0"]
```
